# Optimizing a Trainium2 kernel written in Bass

```python
import jax, jax.numpy as jnp
from jax import lax
import numpy as np

D_MODEL = 1024
BATCH = 1
SEQ = 1024
DEPTH = 2

GRID_W = 64
CTX_LEN = 256
N_MOD = 6
EPS = 1e-6

HEAD_DIM = 64
N_Q_HEADS = 8
N_KV_HEADS = 2
Q_PER_KV = N_Q_HEADS // N_KV_HEADS
ATT_W = N_Q_HEADS * HEAD_DIM
KV_W = N_KV_HEADS * HEAD_DIM
WINDOW = 128
ATT_BLOCK = 128
ROPE_PAIRS = HEAD_DIM // 4
ROPE_BASE = 10000.0

SC_W = D_MODEL // 2
SC_WIDTH = 3
SC_PAD = (SC_WIDTH // 2, SC_WIDTH - 1 - SC_WIDTH // 2)
IN_AB = 2 * KV_W + ATT_W + 3 * SC_W
AB_SPLITS = [KV_W, 2 * KV_W, 2 * KV_W + ATT_W, 2 * KV_W + ATT_W + SC_W, 2 * KV_W + ATT_W + 2 * SC_W]

POOL_W = D_MODEL // 2
POOL_WINDOWS = (2, 4, 8, 16)
POOL_GROUPS = len(POOL_WINDOWS)
POOL_GW = POOL_W // POOL_GROUPS

LRU_W = D_MODEL // 2
LRU_BLOCKS = 8
LRU_BW = LRU_W // LRU_BLOCKS
LRU_CONV = 4
LRU_PAD = (LRU_CONV // 2, LRU_CONV - 1 - LRU_CONV // 2)
LRU_C = 8.0
IN_CD = 2 * LRU_W + POOL_W
CD_SPLITS = [LRU_W, 2 * LRU_W]

MIX_W = D_MODEL

N_GROUPS = 4
EXPERTS_PER_GROUP = 8
N_EXPERTS = N_GROUPS * EXPERTS_PER_GROUP
TOP_K = 2
D_EXPERT = D_MODEL // 2
MOE_BLOCK = 128

kernel_name = "hybrid_diffusion_prefix_backbone"

def rmsnorm(x, g):
    xf = x.astype(jnp.float32)
    y = xf * lax.rsqrt(jnp.mean(xf * xf, axis=-1, keepdims=True) + EPS)
    return (y * g.astype(jnp.float32)).astype(x.dtype)

def modulate(x, g, shift, scale):
    return rmsnorm(x, g) * (1 + scale) + shift

def depthwise_conv(u, w, b, pad):
    y = lax.conv_general_dilated(u, w[:, None, :], window_strides=(1,), padding=[pad],
                                 dimension_numbers=("NWC", "WIO", "NWC"),
                                 feature_group_count=u.shape[-1])
    return y + b

def axial_rope_tables(n_tokens):
    rows = n_tokens // GRID_W
    row = jnp.repeat(jnp.arange(rows), GRID_W)
    col = jnp.tile(jnp.arange(GRID_W), rows)
    inv_freq = ROPE_BASE ** (-jnp.arange(ROPE_PAIRS, dtype=jnp.float32) / ROPE_PAIRS)
    ang = jnp.stack([row, col], axis=-1).astype(jnp.float32)[..., None] * inv_freq
    return jnp.cos(ang), jnp.sin(ang)

def apply_rope(x, cos, sin):
    shp = x.shape
    bshape = (1, shp[1]) + (1,) * (x.ndim - 3) + cos.shape[1:]
    cos, sin = cos.reshape(bshape), sin.reshape(bshape)
    xr = x.astype(jnp.float32).reshape(shp[:-1] + (2, 2, ROPE_PAIRS))
    x1, x2 = xr[..., 0, :], xr[..., 1, :]
    out = jnp.stack([x1 * cos - x2 * sin, x2 * cos + x1 * sin], axis=-2)
    return out.reshape(shp).astype(x.dtype)

def window_attention(q, k, v, kc, vc, sink):
    Bn, L = q.shape[:2]
    nb = L // ATT_BLOCK
    qb = q.reshape(Bn, nb, ATT_BLOCK, N_KV_HEADS, Q_PER_KV, HEAD_DIM)

    def band(t):
        tp = jnp.pad(t, ((0, 0), (ATT_BLOCK, ATT_BLOCK), (0, 0), (0, 0)))
        tp = tp.reshape(Bn, nb + 2, ATT_BLOCK, N_KV_HEADS, HEAD_DIM)
        return jnp.concatenate([tp[:, :-2], tp[:, 1:-1], tp[:, 2:]], axis=2)

    kb, vb = band(k), band(v)
    scale = HEAD_DIM ** -0.5
    s_loc = jnp.einsum("bnqhgd,bnkhd->bnhgqk", qb, kb).astype(jnp.float32) * scale
    s_ctx = jnp.einsum("bnqhgd,bchd->bnhgqc", qb, kc).astype(jnp.float32) * scale
    i = jnp.arange(ATT_BLOCK)[:, None]
    j = jnp.arange(3 * ATT_BLOCK)[None, :]
    kpos = (jnp.arange(nb)[:, None, None] - 1) * ATT_BLOCK + j
    valid = (jnp.abs(i - j + ATT_BLOCK) <= WINDOW) & (kpos >= 0) & (kpos < L)
    s_loc = jnp.where(valid[None, :, None, None], s_loc, -jnp.inf)
    snk = jnp.broadcast_to(sink.astype(jnp.float32).reshape(1, 1, N_KV_HEADS, Q_PER_KV, 1, 1),
                           s_loc.shape[:-1] + (1,))
    p = jax.nn.softmax(jnp.concatenate([s_loc, s_ctx, snk], axis=-1), axis=-1).astype(v.dtype)
    n_loc, n_ctx = 3 * ATT_BLOCK, kc.shape[1]
    o = (jnp.einsum("bnhgqk,bnkhd->bnqhgd", p[..., :n_loc], vb)
         + jnp.einsum("bnhgqc,bchd->bnqhgd", p[..., n_loc:n_loc + n_ctx], vc))
    return o.reshape(Bn, L, ATT_W)

def context_attention(qc, kc, vc, sink):
    Bn, Lc = qc.shape[:2]
    s = jnp.einsum("bqhgd,bkhd->bhgqk", qc, kc).astype(jnp.float32) * HEAD_DIM ** -0.5
    snk = jnp.broadcast_to(sink.astype(jnp.float32).reshape(1, N_KV_HEADS, Q_PER_KV, 1, 1),
                           s.shape[:-1] + (1,))
    p = jax.nn.softmax(jnp.concatenate([s, snk], axis=-1), axis=-1).astype(vc.dtype)
    o = jnp.einsum("bhgqk,bkhd->bqhgd", p[..., :-1], vc)
    return o.reshape(Bn, Lc, ATT_W)

def multiscale_pool(u, w_pool, scale):
    Bn, L, _ = u.shape
    uf = u.astype(jnp.float32)
    cs = jnp.pad(lax.cumsum(uf, axis=1), ((0, 0), (1, 0), (0, 0)))
    t = jnp.arange(L)
    means = []
    for g, w in enumerate(POOL_WINDOWS):
        lo = jnp.clip(t - w // 2, 0, L)
        hi = jnp.clip(t + w - w // 2, 0, L)
        csg = cs[..., g * POOL_GW:(g + 1) * POOL_GW]
        means.append((csg[:, hi] - csg[:, lo]) / (hi - lo).astype(jnp.float32)[None, :, None])
    d = (jnp.concatenate(means, axis=-1) - uf).astype(u.dtype)
    d = d.reshape(Bn, L, POOL_GROUPS, POOL_GW)
    y = jnp.einsum("blgi,gij->blgj", d, w_pool).reshape(Bn, L, POOL_W)
    return y * scale

def rglru_coeffs(u, wa, ba, wx, bx, lam):
    ub = u.reshape(u.shape[:-1] + (LRU_BLOCKS, LRU_BW))
    r = jax.nn.sigmoid((jnp.einsum("blhi,hij->blhj", ub, wa).reshape(u.shape) + ba).astype(jnp.float32))
    gi = jax.nn.sigmoid((jnp.einsum("blhi,hij->blhj", ub, wx).reshape(u.shape) + bx).astype(jnp.float32))
    log_a = -LRU_C * jax.nn.softplus(-lam.astype(jnp.float32)) * r
    a = jnp.exp(log_a)
    b = jnp.sqrt(-jnp.expm1(2 * log_a)) * gi * u.astype(jnp.float32)
    return a, b

def linear_scan(a, b, h0, reverse):
    idx = -1 if reverse else 0
    b = b.at[:, idx].add(a[:, idx] * h0)

    def combine(l, r):
        return l[0] * r[0], r[0] * l[1] + r[1]

    _, h = lax.associative_scan(combine, (a, b), axis=1, reverse=reverse)
    return h

def merge_branches(branches, g_out, w_out):
    splits = list(np.cumsum([br.shape[-1] for br in branches])[:-1])
    gains = jnp.split(g_out, splits)
    y = jnp.concatenate([rmsnorm(br, g) for br, g in zip(branches, gains)], axis=-1)
    return y @ w_out

def expert_dispatch(h, e_idx, w, w1, w3, w2):
    T, D = h.shape
    n = T * TOP_K
    flat_e = e_idx.reshape(-1)
    order = jnp.argsort(flat_e)
    sorted_e = flat_e[order]
    counts = jnp.bincount(flat_e, length=N_EXPERTS)
    padded = (counts + MOE_BLOCK - 1) // MOE_BLOCK * MOE_BLOCK
    pad_end = jnp.cumsum(padded)
    pad_start = pad_end - padded
    seg_start = jnp.cumsum(counts) - counts
    dest_sorted = pad_start[sorted_e] + jnp.arange(n) - seg_start[sorted_e]
    dest = jnp.zeros((n,), jnp.int32).at[order].set(dest_sorted.astype(jnp.int32))
    n_blocks = (n + N_EXPERTS * (MOE_BLOCK - 1) + MOE_BLOCK - 1) // MOE_BLOCK
    n_slots = n_blocks * MOE_BLOCK
    slot_tok = jnp.full((n_slots,), T, jnp.int32).at[dest].set(jnp.arange(n, dtype=jnp.int32) // TOP_K)
    block_e = jnp.minimum(jnp.searchsorted(pad_end, jnp.arange(n_blocks) * MOE_BLOCK, side="right"),
                          N_EXPERTS - 1)
    xs = jnp.concatenate([h, jnp.zeros((1, D), h.dtype)], axis=0)[slot_tok]
    xs = xs.reshape(n_blocks, MOE_BLOCK, D)

    def run_block(args):
        xb, e = args
        return (jax.nn.silu(xb @ w1[e]) * (xb @ w3[e])) @ w2[e]

    ys = lax.map(run_block, (xs, block_e)).reshape(n_slots, D)
    return jnp.einsum("tkd,tk->td", ys[dest].reshape(T, TOP_K, D), w)

def hier_moe(h, gw, gb, ew, eb, w1, w3, w2):
    T = h.shape[0]
    hf = h.astype(jnp.float32)
    p_group = jax.nn.softmax(hf @ gw.astype(jnp.float32) + gb.astype(jnp.float32), axis=-1)
    p_sel, g_idx = lax.top_k(p_group, 1)
    e_logits = (hf @ ew.astype(jnp.float32) + eb.astype(jnp.float32)).reshape(T, N_GROUPS, EXPERTS_PER_GROUP)
    e_logits = jnp.take_along_axis(e_logits, g_idx[:, :, None], axis=1)[:, 0]
    p_top, e_local = lax.top_k(jax.nn.softmax(e_logits, axis=-1), TOP_K)
    w = p_sel * p_top / jnp.sum(p_top, axis=-1, keepdims=True)
    e_idx = g_idx * EXPERTS_PER_GROUP + e_local
    return expert_dispatch(h, e_idx, w.astype(h.dtype), w1, w3, w2)

def even_mixer(h, hc, w_in, q_g, k_g, sink, cw, cb, cos, sin, need_ctx):
    z = h @ w_in
    k, v, q, gb, gc, gx = jnp.split(z, AB_SPLITS, axis=-1)
    zc = hc @ (w_in if need_ctx else w_in[:, :2 * KV_W])
    kc, vc = zc[..., :KV_W], zc[..., KV_W:2 * KV_W]

    def kv_heads(t):
        return t.reshape(t.shape[:-1] + (N_KV_HEADS, HEAD_DIM))

    def q_heads(t):
        return t.reshape(t.shape[:-1] + (N_KV_HEADS, Q_PER_KV, HEAD_DIM))

    q = apply_rope(rmsnorm(q_heads(q), q_g), cos, sin)
    k = apply_rope(rmsnorm(kv_heads(k), k_g), cos, sin)
    kc = rmsnorm(kv_heads(kc), k_g)
    vc = kv_heads(vc)
    att = window_attention(q, k, kv_heads(v), kc, vc, sink)
    conv = gb * depthwise_conv(gc * gx, cw, cb, SC_PAD)
    if not need_ctx:
        return [att, conv], None
    _, _, qc, gbc, gcc, gxc = jnp.split(zc, AB_SPLITS, axis=-1)
    att_c = context_attention(rmsnorm(q_heads(qc), q_g), kc, vc, sink)
    conv_c = gbc * depthwise_conv(gcc * gxc, cw, cb, SC_PAD)
    return [att, conv], [att_c, conv_c]

def odd_mixer(h, hc, w_in, pool_w, pool_scale, conv_w, conv_b, wa, ba, wx, bx, lam, need_ctx):
    z = h @ w_in
    ux, ug, up = jnp.split(z, CD_SPLITS, axis=-1)
    zc = hc @ (w_in if need_ctx else w_in[:, :LRU_W])
    xl = depthwise_conv(ux, conv_w, conv_b, LRU_PAD)
    xc = depthwise_conv(zc[..., :LRU_W], conv_w, conv_b, LRU_PAD)
    h_lat = jnp.zeros(xl.shape, jnp.float32)
    ctx_states = []
    for d, reverse in enumerate((False, True)):
        a_c, b_c = rglru_coeffs(xc, wa[d], ba[d], wx[d], bx[d], lam[d])
        hs_c = linear_scan(a_c, b_c, jnp.zeros_like(b_c[:, 0]), reverse)
        h0 = hs_c[:, 0] if reverse else hs_c[:, -1]
        a_l, b_l = rglru_coeffs(xl, wa[d], ba[d], wx[d], bx[d], lam[d])
        h_lat = h_lat + linear_scan(a_l, b_l, h0, reverse)
        ctx_states.append(hs_c)
    lat = [multiscale_pool(up, pool_w, pool_scale), h_lat.astype(ug.dtype) * jax.nn.gelu(ug)]
    if not need_ctx:
        return lat, None
    _, ugc, upc = jnp.split(zc, CD_SPLITS, axis=-1)
    h_ctx = (ctx_states[0] + ctx_states[1]).astype(ugc.dtype)
    return lat, [multiscale_pool(upc, pool_w, pool_scale), h_ctx * jax.nn.gelu(ugc)]

def setup_inputs(seed: int = 0) -> dict:
    key = jax.random.key(seed)
    ks = iter(jax.random.split(key, 48))
    n_even, n_odd = (DEPTH + 1) // 2, DEPTH // 2

    def nrm(shape, std):
        return std * jax.random.normal(next(ks), shape, jnp.float32)

    def gain(shape):
        return 1.0 + 0.05 * jax.random.normal(next(ks), shape, jnp.float32)

    u = jax.random.uniform(next(ks), (n_odd, 2, LRU_W), jnp.float32, 0.9, 0.999)
    a0 = u ** (1.0 / LRU_C)
    lru_lambda = jnp.log(a0) - jnp.log1p(-a0)
    return {
        "x": nrm((BATCH, SEQ, D_MODEL), 1.0),
        "c": nrm((BATCH, D_MODEL), 1.0),
        "ctx": nrm((BATCH, CTX_LEN, D_MODEL), 1.0),
        "c_ctx": nrm((D_MODEL,), 1.0),
        "ada_w": nrm((DEPTH, D_MODEL, N_MOD * D_MODEL), 0.5 * D_MODEL ** -0.5),
        "ada_b": nrm((DEPTH, N_MOD * D_MODEL), 0.02),
        "norm_mix": gain((DEPTH, D_MODEL)),
        "norm_ffn": gain((DEPTH, D_MODEL)),
        "out_norm": gain((DEPTH, MIX_W)),
        "w_out": nrm((DEPTH, MIX_W, D_MODEL), MIX_W ** -0.5),
        "w_in_ab": nrm((n_even, D_MODEL, IN_AB), D_MODEL ** -0.5),
        "q_norm": gain((n_even, HEAD_DIM)),
        "k_norm": gain((n_even, HEAD_DIM)),
        "attn_sink": nrm((n_even, N_Q_HEADS), 0.5),
        "sconv_w": nrm((n_even, SC_WIDTH, SC_W), SC_WIDTH ** -0.5),
        "sconv_b": nrm((n_even, SC_W), 0.02),
        "w_in_cd": nrm((n_odd, D_MODEL, IN_CD), D_MODEL ** -0.5),
        "pool_w": nrm((n_odd, POOL_GROUPS, POOL_GW, POOL_GW), POOL_GW ** -0.5),
        "pool_scale": gain((n_odd, POOL_W)),
        "lru_conv_w": nrm((n_odd, LRU_CONV, LRU_W), LRU_CONV ** -0.5),
        "lru_conv_b": nrm((n_odd, LRU_W), 0.02),
        "lru_wa": nrm((n_odd, 2, LRU_BLOCKS, LRU_BW, LRU_BW), LRU_BW ** -0.5),
        "lru_ba": nrm((n_odd, 2, LRU_W), 0.02),
        "lru_wx": nrm((n_odd, 2, LRU_BLOCKS, LRU_BW, LRU_BW), LRU_BW ** -0.5),
        "lru_bx": nrm((n_odd, 2, LRU_W), 0.02),
        "lru_lambda": lru_lambda,
        "router_gw": nrm((DEPTH, D_MODEL, N_GROUPS), D_MODEL ** -0.5),
        "router_gb": nrm((DEPTH, N_GROUPS), 0.01),
        "router_ew": nrm((DEPTH, D_MODEL, N_EXPERTS), D_MODEL ** -0.5),
        "router_eb": nrm((DEPTH, N_EXPERTS), 0.01),
        "exp_w1": nrm((DEPTH, N_EXPERTS, D_MODEL, D_EXPERT), D_MODEL ** -0.5),
        "exp_w3": nrm((DEPTH, N_EXPERTS, D_MODEL, D_EXPERT), D_MODEL ** -0.5),
        "exp_w2": nrm((DEPTH, N_EXPERTS, D_EXPERT, D_MODEL), D_EXPERT ** -0.5),
    }

def reference(x, c, ctx, c_ctx, ada_w, ada_b, norm_mix, norm_ffn, out_norm, w_out,
              w_in_ab, q_norm, k_norm, attn_sink, sconv_w, sconv_b,
              w_in_cd, pool_w, pool_scale, lru_conv_w, lru_conv_b, lru_wa, lru_ba, lru_wx, lru_bx, lru_lambda,
              router_gw, router_gb, router_ew, router_eb, exp_w1, exp_w3, exp_w2):
    Bn, L, D = x.shape
    cos, sin = axial_rope_tables(L)
    for i in range(DEPTH):
        need_ctx = i < DEPTH - 1
        j = i // 2
        mod = jnp.split((jax.nn.silu(c) @ ada_w[i] + ada_b[i])[:, None, :], N_MOD, axis=-1)
        mod_c = jnp.split(jax.nn.silu(c_ctx) @ ada_w[i] + ada_b[i], N_MOD, axis=-1)
        h = modulate(x, norm_mix[i], mod[0], mod[1])
        hc = modulate(ctx, norm_mix[i], mod_c[0], mod_c[1])
        if i % 2 == 0:
            lat, cx = even_mixer(h, hc, w_in_ab[j], q_norm[j], k_norm[j], attn_sink[j],
                                 sconv_w[j], sconv_b[j], cos, sin, need_ctx)
        else:
            lat, cx = odd_mixer(h, hc, w_in_cd[j], pool_w[j], pool_scale[j], lru_conv_w[j], lru_conv_b[j],
                                lru_wa[j], lru_ba[j], lru_wx[j], lru_bx[j], lru_lambda[j], need_ctx)
        x = x + mod[2] * merge_branches(lat, out_norm[i], w_out[i])
        tokens = modulate(x, norm_ffn[i], mod[3], mod[4]).reshape(-1, D)
        if need_ctx:
            ctx = ctx + mod_c[2] * merge_branches(cx, out_norm[i], w_out[i])
            hc = modulate(ctx, norm_ffn[i], mod_c[3], mod_c[4])
            tokens = jnp.concatenate([tokens, hc.reshape(-1, D)], axis=0)
        y = hier_moe(tokens, router_gw[i], router_gb[i], router_ew[i], router_eb[i],
                     exp_w1[i], exp_w3[i], exp_w2[i])
        x = x + mod[5] * y[:Bn * L].reshape(Bn, L, D)
        if need_ctx:
            ctx = ctx + mod_c[5] * y[Bn * L:].reshape(ctx.shape)
    return x


_drawn_inputs = setup_inputs


def setup_inputs(seed=0):
    import zlib

    import numpy as np

    out = dict(_drawn_inputs(seed))
    spreads = {}
    factors = {'q_norm': 6.227,
     'k_norm': 6.88,
     'attn_sink': 8.0,
     'sconv_b': 6.119,
     'pool_scale': 21.216,
     'lru_conv_b': 3.641,
     'lru_ba': 64.0,
     'lru_bx': 37.884,
     'router_gb': 18.596,
     'router_eb': 21.019}
    for name, (base, spread) in spreads.items():
        noise = np.random.default_rng([zlib.crc32(name.encode()), seed]).standard_normal(out[name].shape)
        drawn = base * np.exp(spread * noise) if base else spread * noise
        out[name] = __import__('jax').numpy.asarray(drawn.astype(out[name].dtype))
    for name, factor in factors.items():
        out[name] = (out[name] * factor).astype(out[name].dtype)
    return out
```

```python
import numpy as np
from contextlib import ExitStack

import concourse.bass as bass
from concourse import mybir

F32 = mybir.dt.float32
I32 = mybir.dt.int32
ALU = mybir.AluOpType
ACT = mybir.ActivationFunctionType
AX = mybir.AxisListType.X

P = 128
D = 1024
KT = D // P
SEQ, CTX = 1024, 256
LT, CT = SEQ // P, CTX // P
NT = LT + CT
TOK = SEQ + CTX
DEPTH = 2
N_MOD = 6
EPS = 1e-6
GRID_W = 64
HD, NQ, NKV = 64, 8, 2
QPK = NQ // NKV
KV_W = NKV * HD
ATT_W = NQ * HD
SC_W = D // 2
PAIRS = HD // 4
ROPE_BASE = 10000.0
BLK = 128
LOCAL = 3 * BLK
NEG = -1e30
BR = ATT_W // P
POOL_WINDOWS = (2, 4, 8, 16)
LRU_C = 8.0
NG, EPG = 4, 8
NE = NG * EPG
FF = D // 2
FT = FF // P
BIG = 1000.0

CHUNKS = [(0, 512), (512, 512), (1024, 256)]
SC_ROW = 1 + SEQ + 1 + 1 + CTX + 1
LRU_ROW = 2 + SEQ + 1 + 2 + CTX + 1

ROW = {}


def _rows():
    at = 0
    for name, n in (("ada_b", DEPTH * N_MOD * KT), ("norm_mix", DEPTH * KT), ("norm_ffn", DEPTH * KT),
                    ("out_norm", DEPTH * KT), ("sconv_w", 3 * BR), ("sconv_b", BR), ("pool_scale", BR),
                    ("lru_conv_w", 4 * BR), ("lru_conv_b", BR), ("lru_ba", 2 * BR), ("lru_bx", 2 * BR),
                    ("lru_lambda", 2 * BR), ("c", KT), ("c_ctx", KT), ("q_norm", 1), ("k_norm", 1)):
        ROW[name] = at
        at += n
    return at


N_ROWS = _rows()

COL = {}


def _cols():
    at = 0
    for name, n in (("ident", P), ("tri", P), ("ones", P), ("rot", P), ("headsel", 2), ("iota", NE),
                    ("group", NE), ("edges", 4 * 16)):
        COL[name] = at
        at += n
    return at


N_COLS = _cols()


def max_blocks(tiles):
    return (2 * tiles * P + NE * (P - 1)) // P


SLOTS = (max_blocks(NT) + 1) * P


def shape_constants():
    c = np.zeros((P, N_COLS), np.float32)
    i = np.arange(P)
    c[i, COL["ident"] + i] = 1
    c[:, COL["tri"]:COL["tri"] + P] = i[:, None] < i[None, :]
    c[:, COL["ones"]:COL["ones"] + P] = 1
    for base in range(0, P, 2 * PAIRS):
        for j in range(PAIRS):
            c[base + PAIRS + j, COL["rot"] + base + j] = -1
            c[base + j, COL["rot"] + base + PAIRS + j] = 1
    c[i, COL["headsel"] + i // HD] = 1
    c[:, COL["iota"]:COL["iota"] + NE] = np.arange(NE)
    c[:, COL["group"]:COL["group"] + NE] = np.arange(NE) // EPG
    for g, w in enumerate(POOL_WINDOWS):
        t = np.concatenate([np.arange(8), np.arange(SEQ - 8, SEQ)])
        n = np.clip(t + w - w // 2, 0, SEQ) - np.clip(t - w // 2, 0, SEQ)
        c[:, COL["edges"] + 16 * g:COL["edges"] + 16 * g + 16] = np.float32(w) / n.astype(np.float32)
    row, col = np.repeat(np.arange(SEQ // GRID_W), GRID_W), np.tile(np.arange(GRID_W), SEQ // GRID_W)
    freq = (np.float32(ROPE_BASE) ** (-np.arange(PAIRS, dtype=np.float32) / np.float32(PAIRS))).astype(np.float32)
    axis, pair = (i % HD) // (2 * PAIRS), i % PAIRS
    ang = np.where(axis[:, None] == 0, row[None], col[None]).astype(np.float32) * freq[pair][:, None]
    rope = np.stack([np.cos(ang), np.sin(ang)], 1).astype(np.float32)
    q, k = np.arange(BLK)[:, None], np.arange(LOCAL)[None]
    band = np.zeros((P, LT, LOCAL), np.float32)
    for n in range(LT):
        pos = (n - 1) * BLK + k
        ok = (np.abs(q - k + BLK) <= BLK) & (pos >= 0) & (pos < SEQ)
        band[:, n] = np.where(ok, 0, NEG)
    blocks = np.broadcast_to(np.arange(64, dtype=np.float32), (1, 64)).copy()
    return {"k_const": c, "k_rope": rope, "k_band": band, "k_blocks": blocks}


class Chain:

    def __init__(self, engine, sem):
        self.engine, self.sem, self.n = engine, sem, 0

    def step(self, ins):
        self.n += 1
        ins.then_inc(self.sem, 1)
        self.engine.wait_ge(self.sem, self.n)


class Program:
    def __init__(self, nc, ins, out):
        self.nc, self.i, self.out = nc, ins, out
        self.used = {}
        self.layer_sems = []

    def name(self, name):
        n = self.used[name] = self.used.get(name, 0) + 1
        return name if n == 1 else f"{name}_{n}"

    def sb(self, ctx, name, shape, dt=F32):
        return ctx.enter_context(self.nc.sbuf_tensor(self.name(name), shape, dt))

    def ps(self, ctx, name, shape):
        return ctx.enter_context(self.nc.psum_tensor(self.name(name), shape, F32))

    def sem(self, ctx, name):
        sem = self.nc.alloc_semaphore(self.name(name))
        self.layer_sems.append(sem)
        return sem

    def clear_semaphores(self):
        self.nc.clear_and_free_semaphores(self.layer_sems)
        self.nc.all_engine_barrier()
        self.layer_sems = []

    def c(self, name, n=None, parts=P):
        n = P if n is None else n
        return self.const[0:parts, COL[name]:COL[name] + n]

    def param(self, name, k=0):
        return self.cols[:, ROW[name] + k:ROW[name] + k + 1]

    def build(self):
        nc = self.nc
        self.xs = nc.dram_tensor("xs_slots", (SLOTS, D), F32, kind="Internal").ap()
        self.ys = self.xs
        with ExitStack() as top:
            self.const = self.sb(top, "const", [P, N_COLS])
            self.cols = self.sb(top, "cols", [P, N_ROWS])
            self.mods = self.sb(top, "mods", [P, DEPTH, N_MOD, KT, 2])
            self.gain = self.sb(top, "gain", [P, DEPTH, 2, KT, 2])
            self.decay = self.sb(top, "decay", [P, 2, 2 * BR])
            self.slot = self.sb(top, "slot", [P, 2, NT], I32)
            self.wgt = self.sb(top, "wgt", [P, 2, NT])
            self.table = self.sb(top, "table", [1, 64], I32)
            self.xT = self.sb(top, "xT", [P, KT, TOK])
            self.prologue()
            self.layer_even()
            self.feed_forward(0, NT)
            self.clear_semaphores()
            self.layer_odd()
            self.feed_forward(1, LT)
            self.epilogue()

    def prologue(self):
        nc = self.nc
        CW = 512
        NCH = N_MOD * D // CW
        with ExitStack() as ctx:
            rows = [self.sb(ctx, f"rows{i}", [P, P]) for i in range(2)]
            xin = self.sb(ctx, "xin", [P, 2, D])
            NB = 4
            wbuf = self.sb(ctx, "ada_buf", [P, NB, KT, CW])
            silu = self.sb(ctx, "silu_c", [P, KT, 2])
            lam = self.sb(ctx, "lam", [P, 8, 2 * BR])
            pt = [self.ps(ctx, f"pt{i}", [P, 512]) for i in range(4)]
            pr = self.ps(ctx, "pr", [P, 512])
            pa = [pr, self.ps(ctx, "pa1", [P, 512])]
            mrow = self.sb(ctx, "mod_rows", [2, 2, CW])
            s_row, s_re = self.sem(ctx, "s_row"), self.sem(ctx, "s_re")
            pm = [self.ps(ctx, f"pm{i}", [P, 512]) for i in range(DEPTH)]
            s_rows, s_silu, s_cols = self.sem(ctx, "s_rows"), self.sem(ctx, "s_silu"), self.sem(ctx, "s_cols")
            s_const = self.sem(ctx, "s_const")
            s_x = [self.sem(ctx, f"s_x{i}") for i in range(2)]
            s_w = [self.sem(ctx, f"s_w{i}") for i in range(NB)]
            s_rt, s_tp, s_te = self.sem(ctx, "s_rt"), self.sem(ctx, "s_tp"), self.sem(ctx, "s_te")
            s_mod, s_me, s_dve = (self.sem(ctx, n) for n in ("s_mod", "s_me", "s_dve"))
            s_l, s_act = self.sem(ctx, "s_l"), self.sem(ctx, "s_act")
            block = ctx.enter_context(nc.Block())
            N_LOAD = [0]

            @block.scalar
            def _(act):
                act.dma_start(self.const[:], self.i["k_const"]).then_inc(s_const, 16)

                def load_rows(name, src):
                    at, n = ROW[name], src.shape[0]
                    while n:
                        take = min(n, P - at % P)
                        act.dma_start(rows[at // P][at % P:at % P + take, 0:src.shape[1]],
                                      src[0:take, :]).then_inc(s_rows, 16)
                        N_LOAD[0] += 16
                        at, n, src = at + take, n - take, src[take:, :] if n > take else None

                load_rows("ada_b", self.i["ada_b"].rearrange("l (j p) -> (l j) p", p=P))
                load_rows("norm_mix", self.i["norm_mix"].rearrange("l (j p) -> (l j) p", p=P))
                load_rows("norm_ffn", self.i["norm_ffn"].rearrange("l (j p) -> (l j) p", p=P))
                load_rows("out_norm", self.i["out_norm"].rearrange("l (j p) -> (l j) p", p=P))
                load_rows("sconv_w", self.i["sconv_w"].rearrange("a k (j p) -> (a k j) p", p=P))
                load_rows("sconv_b", self.i["sconv_b"].rearrange("a (j p) -> (a j) p", p=P))
                load_rows("pool_scale", self.i["pool_scale"].rearrange("a (j p) -> (a j) p", p=P))
                load_rows("lru_conv_w", self.i["lru_conv_w"].rearrange("a k (j p) -> (a k j) p", p=P))
                load_rows("lru_conv_b", self.i["lru_conv_b"].rearrange("a (j p) -> (a j) p", p=P))
                load_rows("lru_ba", self.i["lru_ba"].rearrange("a k (j p) -> (a k j) p", p=P))
                load_rows("lru_bx", self.i["lru_bx"].rearrange("a k (j p) -> (a k j) p", p=P))
                load_rows("lru_lambda", self.i["lru_lambda"].rearrange("a k (j p) -> (a k j) p", p=P))
                load_rows("c", self.i["c"].rearrange("a (j p) -> (a j) p", p=P))
                load_rows("c_ctx", self.i["c_ctx"].rearrange("(j p) -> j p", p=P))
                for name in ("q_norm", "k_norm"):
                    r = ROW[name]
                    for half in range(2):
                        act.dma_start(rows[r // P][r % P:r % P + 1, HD * half:HD * half + HD],
                                      self.i[name]).then_inc(s_rows, 16)
                        N_LOAD[0] += 16
                act.wait_ge(s_cols, 1)
                for k, name in enumerate(("c", "c_ctx")):
                    act.activation(silu[:, :, k], self.cols[:, ROW[name]:ROW[name] + KT], ACT.Silu).then_inc(s_silu, 1)
                act.wait_ge(s_l, 1)
                act.activation(lam[:, 2, :], lam[:, 1, :], ACT.Exp).then_inc(s_act, 1)
                for t in range(NT):
                    for half in range(2):
                        act.wait_ge(s_tp, 2 * t + half + 1)
                        act.activation(self.xT[:, 4 * half:4 * half + 4, t * P:(t + 1) * P],
                                       pt[2 * (t % 2) + half][:, :].rearrange("p (k c) -> p k c", k=4),
                                       ACT.Copy).then_inc(s_te, 1)
                for n in range(DEPTH * NCH):
                    act.wait_ge(s_row, n + 1)
                    if n >= 2:
                        act.wait_ge(s_mod, n - 1)
                    act.activation(mrow[:, n % 2, :], pa[n % 2][0:2, :], ACT.Copy).then_inc(s_re, 1)

            def load(sp, n):
                layer, ch = divmod(n, NCH)
                sp.dma_start(wbuf[:, n % NB, :, :],
                             self.i["ada_w"][layer, :, ch * CW:(ch + 1) * CW].rearrange("(k p) n -> p k n", p=P)
                             ).then_inc(s_w[n % NB], 16)

            @block.sync
            def _(sp):
                for t in range(NT):
                    if t >= 2:
                        sp.wait_ge(s_tp, 2 * (t - 1))
                    src = self.i["x"][0, t * P:(t + 1) * P, :] if t < LT else self.i["ctx"][0, (t - LT) * P:(t - LT + 1) * P, :]
                    sp.dma_start(xin[:, t % 2, :], src).then_inc(s_x[t % 2], 16)
                    if t < NB:
                        load(sp, t)
                for n in range(NB, DEPTH * NCH):
                    sp.wait_ge(s_row, n - NB + 1)
                    load(sp, n)

            @block.tensor
            def _(pe):
                pe.wait_ge(s_const, 16)
                pe.wait_ge(s_rows, N_LOAD[0])
                for i in range(2):
                    n = min(P, N_ROWS - i * P)
                    pe.transpose(pr[:, i * P:i * P + n], rows[i][0:n, :], self.c("ident", n, n)).then_inc(s_rt, 1)
                for t in range(NT):
                    pe.wait_ge(s_x[t % 2], 16 * (t // 2 + 1))
                    for half in range(2):
                        if t >= 2:
                            pe.wait_ge(s_te, 2 * (t - 2) + half + 1)
                        for k in range(4):
                            ins = pe.transpose(pt[2 * (t % 2) + half][:, k * P:(k + 1) * P],
                                               xin[:, t % 2, (4 * half + k) * P:(4 * half + k + 1) * P], self.c("ident"))
                        ins.then_inc(s_tp, 1)
                pe.wait_ge(s_silu, 2)

                def to_columns(n):
                    layer, ch = divmod(n, NCH)
                    pe.wait_ge(s_re, n + 1)
                    for j in range(CW // P):
                        at = 2 * (ch * (CW // P) + j)
                        ins = pe.transpose(pm[layer][:, at:at + 2], mrow[:, n % 2, j * P:(j + 1) * P],
                                           self.c("ident", 2, 2))
                    ins.then_inc(s_mod, 1)

                for n in range(DEPTH * NCH):
                    pe.wait_ge(s_w[n % NB], 16 * (n // NB + 1))
                    if n >= 2:
                        pe.wait_ge(s_re, n - 1)
                    for k in range(KT):
                        ins = pe.matmul(pa[n % 2][0:2, :], silu[:, k, :], wbuf[:, n % NB, k, :],
                                        start=(k == 0), stop=(k == KT - 1))
                    ins.then_inc(s_row, 1)
                    if n:
                        to_columns(n - 1)
                to_columns(DEPTH * NCH - 1)

            @block.vector
            def _(dve):
                link = Chain(dve, s_dve)
                dve.wait_ge(s_rt, 2)
                dve.tensor_copy(self.cols[:], pr[:, 0:N_ROWS]).then_inc(s_cols, 1)
                dve.wait_ge(s_cols, 1)
                L = self.cols[:, ROW["lru_lambda"]:ROW["lru_lambda"] + 2 * BR]
                link.step(dve.tensor_scalar(lam[:, 0, :], L, -1.0, None, ALU.mult))
                link.step(dve.tensor_tensor(lam[:, 3, :], L, lam[:, 0, :], ALU.min))
                dve.tensor_copy(lam[:, 1, :], lam[:, 3, :]).then_inc(s_l, 1)
                dve.wait_ge(s_act, 1)
                link.step(dve.tensor_scalar(lam[:, 4, :], lam[:, 2, :], 2.0, None, ALU.add))
                link.step(dve.reciprocal(lam[:, 5, :], lam[:, 4, :]))
                link.step(dve.tensor_tensor(lam[:, 5, :], lam[:, 2, :], lam[:, 5, :], ALU.mult))
                link.step(dve.tensor_tensor(lam[:, 6, :], lam[:, 5, :], lam[:, 5, :], ALU.mult))
                link.step(dve.memset(lam[:, 7, :], 1.0 / 17))
                for n in range(7, -1, -1):
                    link.step(dve.tensor_tensor(lam[:, 7, :], lam[:, 7, :], lam[:, 6, :], ALU.mult))
                    link.step(dve.tensor_scalar(lam[:, 7, :], lam[:, 7, :], 1.0 / (2 * n + 1), None, ALU.add))
                link.step(dve.tensor_tensor(lam[:, 7, :], lam[:, 7, :], lam[:, 5, :], ALU.mult))
                link.step(dve.tensor_scalar(lam[:, 0, :], lam[:, 0, :], 0.0, None, ALU.max))
                link.step(dve.scalar_tensor_tensor(lam[:, 0, :], lam[:, 7, :], 2.0, lam[:, 0, :], ALU.mult, ALU.add))
                for s, sign in enumerate((-1.0, 1.0)):
                    link.step(dve.tensor_scalar(self.decay[:, s, :], lam[:, 0, :], sign * LRU_C, None, ALU.mult))
                link.step(dve.tensor_scalar(self.param("q_norm"), self.param("q_norm"), HD ** -0.5, None, ALU.mult))
                for layer in range(DEPTH):
                    dve.wait_ge(s_mod, (layer + 1) * NCH)
                    m = self.mods[:, layer, :, :, :].rearrange("p a k s -> p (a k) s")
                    b = self.cols[:, ROW["ada_b"] + layer * N_MOD * KT:ROW["ada_b"] + (layer + 1) * N_MOD * KT]
                    dve.tensor_tensor(m, pm[layer][:, 0:2 * N_MOD * KT].rearrange("p (a s) -> p a s", s=2),
                                      b.unsqueeze(2).to_broadcast([P, N_MOD * KT, 2]), ALU.add).then_inc(s_me, 1)
                    dve.wait_ge(s_me, layer + 1)
                    for w, (which, name) in enumerate(((1, "norm_mix"), (4, "norm_ffn"))):
                        g = self.cols[:, ROW[name] + layer * KT:ROW[name] + (layer + 1) * KT]
                        link.step(dve.tensor_scalar(self.gain[:, layer, w, :, :], self.mods[:, layer, which, :, :], 1.0,
                                                    None, ALU.add))
                        link.step(dve.tensor_tensor(self.gain[:, layer, w, :, :], self.gain[:, layer, w, :, :],
                                                    g.unsqueeze(2).to_broadcast([P, KT, 2]), ALU.mult))

    def norm_open(self, ctx, tag, nt):
        n = dict(nt=nt, tok=nt * P)
        for name in ("sq", "sum", "var", "std", "rstd", "bc", "x", "h"):
            n[name] = self.sem(ctx, f"{tag}_{name}")
        n["rows"] = self.sb(ctx, f"{tag}_rows", [P, 4, NT])
        return n

    def norm_act(self, act, n, hT, layer, which):
        tok = n["tok"]
        for k in range(KT):
            act.activation(hT[:, k, 0:tok], self.xT[:, k, 0:tok], ACT.Square).then_inc(n["sq"], 1)
        act.wait_ge(n["var"], 1)
        act.activation(n["rows"][:, 1, 0:n["nt"]], n["rows"][:, 0, 0:n["nt"]], ACT.Sqrt).then_inc(n["std"], 1)
        for k in range(KT):
            act.wait_ge(n["x"], k + 1)
            for s, (at, m) in enumerate(((0, SEQ), (SEQ, CTX))):
                if at < tok:
                    ins = act.activation(hT[:, k, at:at + m], hT[:, k, at:at + m], ACT.Identity,
                                         bias=self.mods[:, layer, 3 * which, k, s:s + 1],
                                         scale=self.gain[:, layer, which, k, s:s + 1])
            ins.then_inc(n["h"], 1)

    def norm_pe(self, pe, n, hT, ps_sum, ps_bc):
        for t in range(n["nt"]):
            for k in range(KT):
                if t == 0:
                    pe.wait_ge(n["sq"], k + 1)
                ins = pe.matmul(ps_sum[:, t:t + 1], hT[:, k, t * P:(t + 1) * P], self.c("ones", 1),
                                start=(k == 0), stop=(k == KT - 1))
        ins.then_inc(n["sum"], 1)
        pe.wait_ge(n["rstd"], 1)
        for t in range(n["nt"]):
            ins = pe.transpose(ps_bc[:, t * P:(t + 1) * P],
                               n["rows"][:, 3, t:t + 1].to_broadcast([P, P]), self.c("ident"))
        ins.then_inc(n["bc"], 1)

    def norm_dve(self, dve, n, hT, ps_sum, ps_bc):
        nt, tok = n["nt"], n["tok"]
        dve.wait_ge(n["sum"], 1)
        dve.tensor_scalar(n["rows"][:, 0, 0:nt], ps_sum[:, 0:nt], 1.0 / D, EPS, ALU.mult, ALU.add).then_inc(n["var"], 1)
        dve.wait_ge(n["std"], 1)
        dve.reciprocal(n["rows"][:, 3, 0:nt], n["rows"][:, 1, 0:nt]).then_inc(n["rstd"], 1)
        dve.wait_ge(n["bc"], 1)
        for k in range(KT):
            dve.tensor_tensor(hT[:, k, 0:tok], self.xT[:, k, 0:tok], ps_bc[:, 0:tok], ALU.mult).then_inc(n["x"], 1)

    def layer_even(self):
        with ExitStack() as ctx:
            self.Y = self.sb(ctx, "Y", [P, 2 * BR, TOK])
            with ExitStack() as qkv:
                self.qT = self.sb(qkv, "qT", [P, BR, TOK])
                self.kT = self.sb(qkv, "kT", [P, NKV, BLK + SEQ + BLK + CTX])
                self.v = self.sb(qkv, "v_rows", [P, 1 + LT + 1 + CT, KV_W])
                self.even_projections()
                self.attention()
            self.merge(0, NT)

    def even_projections(self):
        nc = self.nc
        WC = 3 * P
        tiles = [("k", 0), ("k", 1), ("v", 0)] + [("q", i) for i in range(BR)]
        chunk_of = [(0, 0), (0, 1), (0, 2), (1, 0), (1, 1), (2, 0), (2, 1)]
        for i in range(BR):
            tiles += [("gc", i), ("gx", i), ("gb", i)]
            chunk_of += [(3 + i, 0), (3 + i, 1), (3 + i, 2)]
        NCHUNK = 3 + BR
        NC = len(CHUNKS)
        normed = [m for m, (kind, _) in enumerate(tiles) if kind in "kq"]
        K_COL = lambda at: BLK + at if at < SEQ else BLK + SEQ + BLK + at - SEQ
        with ExitStack() as ctx:
            hT = self.sb(ctx, "hT", [P, KT, TOK])
            w = self.sb(ctx, "w_ab", [P, 2, KT, WC])
            rope = self.sb(ctx, "rope", [P, 2, SEQ])
            raws, sqs = [self.Y[:, n, :] for n in (0, 1)], [self.Y[:, n, :] for n in (2, 3)]
            ta = self.sb(ctx, "ta", [P, SC_ROW])
            u = self.sb(ctx, "u", [P, SC_ROW])
            spread = tb = u[:, 0:TOK]
            hrow = self.sb(ctx, "head_rows", [P, 3, 2 * NT])
            z = [self.ps(ctx, f"z{i}", [P, 512]) for i in range(2)]
            bc = self.ps(ctx, "bc", [P, 3 * 512])
            rt = [self.ps(ctx, f"rt{i}", [P, 512]) for i in range(2)]
            ssum = self.ps(ctx, "ssum", [P, 512])
            nrm = self.norm_open(ctx, "n0", NT)
            s_w = [self.sem(ctx, f"s_w{i}") for i in range(2)]
            (s_rope, s_z, s_raw, s_rawfree, s_hs, s_hv, s_hd, s_hr, s_hb, s_n, s_rot, s_ta, s_tb, s_done,
             s_vt, s_v, s_gc, s_u, s_cv, s_y, s_pad, s_zf, s_zs, s_rc) = (
                self.sem(ctx, "s_" + n) for n in (
                    "rope", "z", "raw", "rawfree", "hs", "hv", "hd", "hr", "hb", "n", "rot", "ta", "tb", "done",
                    "vt", "v", "gc", "u", "cv", "y", "pad", "zf", "zs", "rc"))
            zero = self.sb(ctx, "zero", [P, D // 2])
            block = ctx.enter_context(nc.Block())
            W = self.i["w_in_ab"][0].rearrange("(k p) n -> p k n", p=P)
            Q0 = 2 * KV_W
            B0, C0, X0 = Q0 + ATT_W, Q0 + ATT_W + SC_W, Q0 + ATT_W + 2 * SC_W

            unit = [(m, c) for m in range(len(tiles)) for c in range(NC)]
            raw_of = {m: n for n, m in enumerate(m for m, (kind, _) in enumerate(tiles) if kind in "kqv")}

            def wait_z_read(eng, n):
                m, c = unit[n]
                kind, i = tiles[m]
                if kind in "kqv":
                    eng.wait_ge(s_raw, NC * raw_of[m] + c + 1)
                else:
                    eng.wait_ge({"gc": s_gc, "gx": s_u, "gb": s_y}[kind], NC * i + c + 1)

            arrived = []

            @block.sync
            def _(sp):
                sp.dma_start(rope[:], self.i["k_rope"]).then_inc(s_rope, 16)
                done = [0, 0]
                for ch in range(NCHUNK):
                    b = ch % 2
                    if ch >= 2:
                        last = max(m for m in range(len(tiles)) if chunk_of[m][0] == ch - 2)
                        sp.wait_ge(s_z, NC * (last + 1))
                    if ch == 0:
                        parts = [(j * P + h * HD, j * HD, HD) for j in range(2) for h in range(2)] + [(2 * P, KV_W, P)]
                    elif ch < 3:
                        parts = [(0, Q0 + (ch - 1) * 2 * P, 2 * P)]
                    else:
                        parts = [(g * P, base + (ch - 3) * P, P) for g, base in enumerate((C0, X0, B0))]
                    for to, at, n in parts:
                        sp.dma_start(w[:, b, :, to:to + n], W[:, :, at:at + n]).then_inc(s_w[b], 16)
                        done[b] += 16
                    arrived.append(done[b])

            @block.tensor
            def _(pe):
                self.norm_pe(pe, nrm, hT, ssum, bc)
                posts = []

                def head_sums(m):
                    n = normed.index(m)
                    pe.wait_ge(s_raw, NC * raw_of[m] + NC)
                    if n:
                        pe.wait_ge(s_hv, n)
                    for t in range(NT):
                        ins = pe.matmul(ssum[:, 2 * t:2 * t + 2], sqs[raw_of[m] % 2][:, t * P:(t + 1) * P], self.c("headsel", 2),
                                        start=True, stop=True)
                    ins.then_inc(s_hs, 1)

                def head_spread(m):
                    n = normed.index(m)
                    pe.wait_ge(s_hr, n + 1)
                    for t in range(NT):
                        ins = pe.transpose(bc[:, t * P:(t + 1) * P],
                                           spread[:, t * P:(t + 1) * P], self.c("ident"))
                    ins.then_inc(s_hb, 1)

                def rotate(m):
                    kind, i = tiles[m]
                    n = normed.index(m)
                    pe.wait_ge(s_n, n + 1)
                    if n:
                        pe.wait_ge(s_tb, n)
                    for c in range(2):
                        src = self.qT[:, i, c * 512:(c + 1) * 512] if kind == "q" else self.kT[:, i, BLK + c * 512:BLK + (c + 1) * 512]
                        ins = pe.matmul(rt[c][:], self.c("rot"), src, start=True, stop=True)
                    ins.then_inc(s_rot, 1)

                def v_rows(m):
                    pe.wait_ge(s_raw, NC * raw_of[m] + NC)
                    n = sum(1 for x in normed if x < m)
                    pe.wait_ge(s_n, n)
                    for t in range(NT):
                        ins = pe.transpose(bc[:, t * P:(t + 1) * P], raws[raw_of[m] % 2][:, t * P:(t + 1) * P],
                                           self.c("ident"))
                    ins.then_inc(s_vt, 1)

                for n, (m, c) in enumerate(unit):
                    if c == 0 and (m == 0 or chunk_of[m][0] != chunk_of[m - 1][0]):
                        ch = chunk_of[m][0]
                        pe.wait_ge(s_w[ch % 2], arrived[ch])
                    if n >= 2:
                        wait_z_read(pe, n - 2)
                    at, size = CHUNKS[c]
                    for k in range(KT):
                        if n == 0:
                            pe.wait_ge(nrm["h"], k + 1)
                        to = chunk_of[m][1] * P
                        ins = pe.matmul(z[n % 2][:, 0:size], w[:, chunk_of[m][0] % 2, k, to:to + P], hT[:, k, at:at + size],
                                        start=(k == 0), stop=(k == KT - 1))
                    ins.then_inc(s_z, 1)
                    if m:
                        kind = tiles[m - 1][0]
                        if kind in "kq":
                            (head_sums, head_spread, rotate)[c](m - 1)
                        elif kind == "v" and c == 0:
                            v_rows(m - 1)

            @block.scalar
            def _(act):
                self.norm_act(act, nrm, hT, 0, 0)
                sent = 0
                for n, (m, c) in enumerate(unit):
                    kind, i = tiles[m]
                    at, size = CHUNKS[c]
                    if kind in "kqv":
                        r = raw_of[m]
                        act.wait_ge(s_z, n + 1)
                        if r >= 2 and c == 0:
                            act.wait_ge(s_rawfree, r - 1)
                        raw, sq = raws[r % 2], sqs[r % 2]
                        if kind != "v":
                            act.activation(sq[:, at:at + size], z[n % 2][:, 0:size], ACT.Square)
                        act.activation(raw[:, at:at + size], z[n % 2][:, 0:size], ACT.Copy).then_inc(s_raw, 1)
                    elif kind == "gc":
                        act.wait_ge(s_z, n + 1)
                        if i:
                            act.wait_ge(s_u, NC * (i - 1) + c + 1)
                        elif c == 0:
                            act.wait_ge(s_rawfree, len(raw_of) - 1)
                        act.activation(raws[1][:, at:at + size], z[n % 2][:, 0:size], ACT.Copy).then_inc(s_gc, 1)
                    if m and c == 1 and tiles[m - 1][0] in "kq":
                        e = normed.index(m - 1)
                        act.wait_ge(s_hv, e + 1)
                        act.activation(hrow[:, 1, :], hrow[:, 0, :], ACT.Sqrt).then_inc(s_hd, 1)
                    if m and c == 1 and tiles[m - 1][0] == "v":
                        act.wait_ge(s_vt, 1)
                        act.wait_ge(s_pad, 1)
                        act.activation(self.v[:, 1:1 + LT, :], bc[:, 0:SEQ].rearrange("p (t c) -> p t c", c=P), ACT.Copy)
                        act.activation(self.v[:, 2 + LT:, :], bc[:, SEQ:TOK].rearrange("p (t c) -> p t c", c=P),
                                       ACT.Copy).then_inc(s_v, 1)

            @block.vector
            def _(dve):
                dve.memset(self.kT[:, :, 0:BLK], 0.0)
                dve.memset(self.kT[:, :, BLK + SEQ:BLK + SEQ + BLK], 0.0)
                dve.memset(self.v[:, 0, :], 0.0)
                dve.memset(self.v[:, 1 + LT, :], 0.0).then_inc(s_pad, 1)
                dve.memset(zero[:], 0.0).then_inc(s_zf, 1)
                self.norm_dve(dve, nrm, hT, ssum, bc)
                dve.wait_ge(s_rope, 16)
                link = Chain(dve, s_cv)
                for n, (m, c) in enumerate(unit):
                    kind, i = tiles[m]
                    at, size = CHUNKS[c]
                    if kind == "gx":
                        dve.wait_ge(s_gc, NC * i + c + 1)
                        dve.wait_ge(s_z, n + 1)
                        to = 1 + at if at < SEQ else 3 + at
                        dve.tensor_tensor(u[:, to:to + size], raws[1][:, at:at + size], z[n % 2][:, 0:size], ALU.mult).then_inc(s_u, 1)
                        if c == NC - 1:
                            dve.wait_ge(s_u, NC * (i + 1))
                            L = SC_ROW - 2
                            link.step(dve.tensor_scalar(ta[:, 0:L], u[:, 0:L], self.param("sconv_w", i), self.param("sconv_b", i),
                                                        ALU.mult, ALU.add))
                            for k in (1, 2):
                                link.step(dve.scalar_tensor_tensor(ta[:, 0:L], u[:, k:k + L], self.param("sconv_w", k * BR + i),
                                                                   ta[:, 0:L], ALU.mult, ALU.add))
                    elif kind == "gb":
                        dve.wait_ge(s_z, n + 1)
                        src = at if at < SEQ else 2 + at
                        dve.tensor_tensor(self.Y[:, BR + i, at:at + size], ta[:, src:src + size], z[n % 2][:, 0:size],
                                          ALU.mult).then_inc(s_y, 1)
                        if c == NC - 1:
                            dve.wait_ge(s_y, NC * (i + 1))
                    if m and tiles[m - 1][0] in "kq":
                        e = normed.index(m - 1)
                        pk, pi = tiles[m - 1]
                        raw = raws[raw_of[m - 1] % 2]
                        if c == 0:
                            dve.wait_ge(s_hs, e + 1)
                            dve.tensor_scalar(hrow[:, 0, :], ssum[:, 0:2 * NT], 1.0 / HD, EPS, ALU.mult, ALU.add).then_inc(s_hv, 1)
                        elif c == 1:
                            dve.wait_ge(s_hd, e + 1)
                            dve.reciprocal(hrow[:, 2, :], hrow[:, 1, :]).then_inc(s_rc, 1)
                            dve.wait_ge(s_rc, e + 1)
                            dve.tensor_copy(spread.rearrange("p (t c) -> p t c", c=HD),
                                            hrow[:, 2, :].unsqueeze(2).to_broadcast([P, 2 * NT, HD])).then_inc(s_hr, 1)
                            dve.wait_ge(s_hb, e + 1)
                            gain = self.param("q_norm" if pk == "q" else "k_norm")
                            if pk == "q":
                                dve.scalar_tensor_tensor(self.qT[:, pi, :], raw, gain, bc[:, 0:TOK], ALU.mult, ALU.mult
                                                         ).then_inc(s_n, 1)
                            else:
                                dve.scalar_tensor_tensor(self.kT[:, pi, BLK:BLK + SEQ], raw[:, 0:SEQ], gain, bc[:, 0:SEQ],
                                                         ALU.mult, ALU.mult)
                                dve.scalar_tensor_tensor(self.kT[:, pi, 2 * BLK + SEQ:], raw[:, SEQ:TOK], gain,
                                                         bc[:, SEQ:TOK], ALU.mult, ALU.mult).then_inc(s_n, 1)
                            dve.wait_ge(s_n, e + 1)
                            dve.engine_nop().then_inc(s_rawfree, 1)
                        else:
                            dve.wait_ge(s_rot, e + 1)
                            for h in range(2):
                                ins = dve.tensor_tensor(tb[:, h * 512:(h + 1) * 512], rt[h][:], rope[:, 1, h * 512:(h + 1) * 512],
                                                        ALU.mult)
                            ins.then_inc(s_tb, 1)
                            dve.wait_ge(s_tb, e + 1)
                            dve.wait_ge(s_ta, e + 1)
                            dst = self.qT[:, pi, 0:SEQ] if pk == "q" else self.kT[:, pi, BLK:BLK + SEQ]
                            dve.tensor_tensor(dst, ta[:, 0:SEQ], tb[:, 0:SEQ], ALU.add).then_inc(s_done, 1)
                            dve.wait_ge(s_done, e + 1)
                            if e == len(normed) - 1:
                                link.step(dve.memset(u[:], 0.0))
                    if m and c == 1 and tiles[m - 1][0] == "v":
                        dve.wait_ge(s_v, 1)
                        dve.engine_nop().then_inc(s_rawfree, 1)

            @block.gpsimd
            def _(pool):
                pool.wait_ge(s_zf, 1)
                for b in range(SLOTS // P):
                    for h in range(2):
                        pool.dma_start(self.xs[b * P:(b + 1) * P, h * D // 2:(h + 1) * D // 2], zero[:]).then_inc(s_zs, 16)
                for e, m in enumerate(normed):
                    kind, i = tiles[m]
                    pool.wait_ge(s_n, e + 1)
                    if e == 0:
                        pool.wait_ge(s_rope, 16)
                    if e:
                        pool.wait_ge(s_done, e)
                    src = self.qT[:, i, 0:SEQ] if kind == "q" else self.kT[:, i, BLK:BLK + SEQ]
                    pool.tensor_tensor(ta[:, 0:SEQ], src, rope[:, 0, :], ALU.mult).then_inc(s_ta, 1)
                pool.wait_ge(s_zs, 32 * (SLOTS // P))

    def attention(self):
        nc = self.nc
        SP_N = LOCAL + CTX
        CREDIT = 2
        with ExitStack() as ctx:
            band = self.sb(ctx, "band", [P, LT * LOCAL])
            sink = self.sb(ctx, "sink", [P, NQ])
            qb = self.sb(ctx, "q_block", [P, BR, BLK])
            kb = self.sb(ctx, "k_block", [P, NKV, LOCAL])
            mask = self.sb(ctx, "mask", [P, LOCAL])
            S = self.sb(ctx, "scores", [P, 2, LOCAL])
            Pr = self.sb(ctx, "probs", [P, 2, SP_N])
            PT = self.sb(ctx, "probsT", [P, 2, SP_N])
            mx = self.sb(ctx, "mx", [P, NQ, 4])
            den = self.sb(ctx, "den", [P, NQ, 4])
            rden = self.sb(ctx, "rden", [P, NQ])
            orow = self.sb(ctx, "o_rows", [P, ATT_W])
            pl = [self.ps(ctx, f"pl{i}", [P, 512]) for i in range(2)]
            pc = [self.ps(ctx, f"pc{i}", [P, 512]) for i in range(2)]
            ptl, ptc = self.ps(ctx, "ptl", [P, 512]), self.ps(ctx, "ptc", [P, 512])
            po, pot = self.ps(ctx, "po", [P, 512]), self.ps(ctx, "pot", [P, 512])
            (s_in, s_q, s_sc, s_m1, s_mx, s_ex, s_ptl, s_ptc, s_pel, s_pec, s_pv, s_rd, s_or, s_ot, s_y, s_snk, s_mm,
             s_dn, s_msk) = (
                self.sem(ctx, "t_" + n) for n in ("in", "q", "sc", "m1", "mx", "ex", "ptl", "ptc", "pel", "pec", "pv", "rd",
                                                  "or", "ot", "y", "snk", "mm", "dn", "msk"))
            block = ctx.enter_context(nc.Block())

            @block.sync
            def _(sp):
                sp.dma_start(band[:], self.i["k_band"].rearrange("p n k -> p (n k)")).then_inc(s_in, 16)
                sp.dma_start(sink[:], self.i["attn_sink"].to_broadcast([P, NQ])).then_inc(s_in, 16)

            def pe_block(pe, n, unit, local):
                pe.wait_ge(s_q, n + 1)
                for h in range(NQ + 1):
                    if h < NQ:
                        g, t, half = h // QPK, h // 2, h % 2
                        lo, hi = half * HD, half * HD + HD
                        pe.wait_ge(s_ex, unit + h + 1)
                        if local:
                            pe.matmul(pl[h % 2][:, 0:LOCAL], qb[lo:hi, t, :],
                                      kb[lo:hi, g, :], start=True, stop=True)
                        pe.matmul(pc[h % 2][:, 0:CTX], qb[lo:hi, t, :], self.kT[lo:hi, g, 2 * BLK + SEQ:],
                                  start=True, stop=True).then_inc(s_sc, 1)
                    if h:
                        u, b, g = unit + h - 1, (h - 1) % 2, (h - 1) // QPK
                        pe.wait_ge(s_ex, CREDIT + u + 1)
                        if local:
                            pe.wait_ge(s_pel, u + 1)
                            for j in range(3):
                                ins = pe.transpose(ptl[:, j * P:(j + 1) * P], Pr[:, b, j * P:(j + 1) * P], self.c("ident"))
                            ins.then_inc(s_ptl, 1)
                        pe.wait_ge(s_pec, u + 1)
                        for j in range(CT):
                            ins = pe.transpose(ptc[:, j * P:(j + 1) * P], Pr[:, b, LOCAL + j * P:LOCAL + (j + 1) * P],
                                               self.c("ident"))
                        ins.then_inc(s_ptc, 1)
                        out = po[:, (h - 1) * HD:h * HD]
                        if h == 1:
                            pe.wait_ge(s_or, n + 1)
                        if local:
                            pe.wait_ge(s_pel, u + 2)
                            for j in range(3):
                                pe.matmul(out, PT[:, b, j * P:(j + 1) * P],
                                          self.v[:, bass.ds(n + j, 1), g * HD:(g + 1) * HD].squeeze(1) if not isinstance(n, int)
                                          else self.v[:, n + j, g * HD:(g + 1) * HD], start=(j == 0), stop=False)
                        pe.wait_ge(s_pec, u + 2)
                        for j in range(CT):
                            ins = pe.matmul(out, PT[:, b, LOCAL + j * P:LOCAL + (j + 1) * P],
                                            self.v[:, 2 + LT + j, g * HD:(g + 1) * HD],
                                            start=(not local and j == 0), stop=(j == CT - 1))
                        ins.then_inc(s_pv, 1)
                pe.wait_ge(s_or, n + 2)
                pe.wait_ge(s_y, n + 1)
                for j in range(BR):
                    ins = pe.transpose(pot[:, j * P:(j + 1) * P], orow[:, j * P:(j + 1) * P], self.c("ident"))
                ins.then_inc(s_ot, 1)

            @block.tensor
            def _(pe):
                pe.sem_inc(s_ptc, CREDIT)
                pe.sem_inc(s_pv, CREDIT)
                with pe.Fori(0, LT) as n:
                    pe_block(pe, n, n * NQ, True)
                for n in range(LT, NT):
                    pe_block(pe, n, n * NQ, False)

            def dve_block(dve, n, unit, local):
                dve.wait_ge(s_ot, n)
                if local:
                    dve.tensor_copy(mask[:], band[:, bass.ds(n * LOCAL, LOCAL)]).then_inc(s_msk, 1)
                    dve.wait_ge(s_msk, n + 1)
                    dve.tensor_copy(kb[:], self.kT[:, :, bass.ds(n * BLK, LOCAL)])
                dve.tensor_copy(qb[:], self.qT[:, :, bass.ds(n * BLK, BLK)]).then_inc(s_q, 1)
                for h in range(NQ + 1):
                    if h < NQ:
                        u, b = unit + h, h % 2
                        dve.wait_ge(s_sc, u + 1)
                        if local:
                            dve.wait_ge(s_ex, u + 1)
                            dve.reduce_max(mx[:, h, 1:2], pc[b][:, 0:CTX], AX)
                            dve.tensor_tensor_reduce(out=S[:, b, :], in0=pl[b][:, 0:LOCAL],
                                                     in1=mask[:], scale=1.0,
                                                     scalar=sink[:, h:h + 1], op0=ALU.add, op1=ALU.max,
                                                     accum_out=mx[:, h, 0:1]).then_inc(s_m1, 1)
                            dve.wait_ge(s_m1, u + 1)
                            dve.tensor_scalar(mx[:, h, 3:4], mx[:, h, 0:1], mx[:, h, 1:2], -1.0, ALU.max, ALU.mult
                                              ).then_inc(s_mx, 1)
                        else:
                            dve.reduce_max(mx[:, h, 1:2], pc[b][:, 0:CTX], AX).then_inc(s_m1, 1)
                            dve.wait_ge(s_m1, u + 1)
                            dve.tensor_scalar(mx[:, h, 3:4], sink[:, h:h + 1], mx[:, h, 1:2], -1.0, ALU.max, ALU.mult
                                              ).then_inc(s_mx, 1)
                    if h and local:
                        u, b = unit + h - 1, (h - 1) % 2
                        dve.wait_ge(s_ptl, u + 1)
                        dve.wait_ge(s_pv, u + 1)
                        dve.tensor_copy(PT[:, b, 0:LOCAL], ptl[:, 0:LOCAL]).then_inc(s_pel, 1)
                dve.wait_ge(s_snk, n + 1)
                dve.tensor_reduce(den[:, :, 3], den[:, :, (0 if local else 1):3], AX, ALU.add).then_inc(s_dn, 1)
                dve.wait_ge(s_dn, n + 1)
                dve.reciprocal(rden[:], den[:, :, 3]).then_inc(s_rd, 1)
                dve.wait_ge(s_rd, n + 1)
                dve.wait_ge(s_pv, CREDIT + unit + NQ)
                dve.tensor_tensor(orow[:].rearrange("p (h c) -> p h c", h=NQ), po[:, :].rearrange("p (h c) -> p h c", h=NQ),
                                  rden[:].unsqueeze(2).to_broadcast([P, NQ, HD]), ALU.mult).then_inc(s_or, 1)

            @block.vector
            def _(dve):
                dve.sem_inc(s_pel, 1)
                dve.sem_inc(s_or, 1)
                dve.memset(den[:], 0.0).then_inc(s_mm, 1)
                dve.wait_ge(s_in, 32)
                with dve.Fori(0, LT) as n:
                    dve_block(dve, n, n * NQ, True)
                for n in range(LT, NT):
                    dve_block(dve, n, n * NQ, False)

            def act_block(act, n, unit, local):
                for h in range(NQ + 1):
                    if h < NQ:
                        u, b = unit + h, h % 2
                        act.wait_ge(s_mx, u + 1)
                        act.wait_ge(s_ptc, u + 1)
                        if local:
                            act.activation(Pr[:, b, 0:LOCAL], S[:, b, :], ACT.Exp, bias=mx[:, h, 3:4],
                                           accum_out=den[:, h, 0:1])
                        act.activation(Pr[:, b, LOCAL:], pc[b][:, 0:CTX], ACT.Exp, bias=mx[:, h, 3:4],
                                       accum_out=den[:, h, 1:2]).then_inc(s_ex, 1)
                        ins = act.activation(den[:, h, 2:3], sink[:, h:h + 1], ACT.Exp, bias=mx[:, h, 3:4])
                        if h == NQ - 1:
                            ins.then_inc(s_snk, 1)
                    if h:
                        u, b = unit + h - 1, (h - 1) % 2
                        act.wait_ge(s_ptc, CREDIT + u + 1)
                        act.wait_ge(s_pv, u + 1)
                        act.activation(PT[:, b, LOCAL:], ptc[:, 0:CTX], ACT.Copy).then_inc(s_pec, 1)
                act.wait_ge(s_ot, n + 1)
                act.activation(self.Y[:, 0:BR, bass.ds(n * BLK, BLK)], pot[:, :].rearrange("p (j c) -> p j c", j=BR),
                               ACT.Copy).then_inc(s_y, 1)

            @block.scalar
            def _(act):
                act.sem_inc(s_pec, 1)
                act.sem_inc(s_y, 1)
                act.sem_inc(s_ex, CREDIT)
                act.wait_ge(s_in, 32)
                act.wait_ge(s_mm, 1)
                with act.Fori(0, LT) as n:
                    act_block(act, n, n * NQ, True)
                for n in range(LT, NT):
                    act_block(act, n, n * NQ, False)

    def merge(self, layer, nt):
        nc = self.nc
        tok = nt * P
        chunks = [(a, n) for a, n in CHUNKS if a < tok]
        NC = len(chunks)
        with ExitStack() as ctx:
            w = self.sb(ctx, "w_o", [P, 2 * BR, D])
            sq = self.sb(ctx, "sq", [P, 2 * BR, tok])
            rows = self.sb(ctx, "rows", [P, 3, 2, NT])
            bc = self.ps(ctx, "bc", [P, 3 * 512])
            z = [self.ps(ctx, f"z{i}", [P, 512]) for i in range(4)]
            ssum = self.ps(ctx, "ssum", [P, 512])
            s_w, s_sq, s_sum, s_var, s_std, s_r, s_bc, s_n, s_z, s_x = (
                self.sem(ctx, "m_" + n) for n in ("w", "sq", "sum", "var", "std", "r", "bc", "n", "z", "x"))
            block = ctx.enter_context(nc.Block())

            @block.sync
            def _(sp):
                for k in range(2):
                    sp.dma_start(w[:, :, k * 512:(k + 1) * 512],
                                 self.i["w_out"][layer, :, k * 512:(k + 1) * 512].rearrange("(k p) n -> p k n", p=P)
                                 ).then_inc(s_w, 16)

            @block.scalar
            def _(act):
                for k in range(2 * BR):
                    act.activation(sq[:, k, :], self.Y[:, k, 0:tok], ACT.Square).then_inc(s_sq, 1)
                for br in range(2):
                    act.wait_ge(s_var, br + 1)
                    act.activation(rows[:, 1, br, 0:nt], rows[:, 0, br, 0:nt], ACT.Sqrt).then_inc(s_std, 1)

            @block.tensor
            def _(pe):
                for br in range(2):
                    if br:
                        pe.wait_ge(s_var, 1)
                    for t in range(nt):
                        for k in range(BR):
                            if t == 0:
                                pe.wait_ge(s_sq, br * BR + k + 1)
                            ins = pe.matmul(ssum[:, t:t + 1], sq[:, br * BR + k, t * P:(t + 1) * P], self.c("ones", 1),
                                            start=(k == 0), stop=(k == BR - 1))
                    ins.then_inc(s_sum, 1)
                for br in range(2):
                    pe.wait_ge(s_r, br + 1)
                    if br:
                        pe.wait_ge(s_n, BR)
                    for t in range(nt):
                        ins = pe.transpose(bc[:, t * P:(t + 1) * P], rows[:, 2, br, t:t + 1].to_broadcast([P, P]),
                                           self.c("ident"))
                    ins.then_inc(s_bc, 1)
                pe.wait_ge(s_w, 32)
                for n in range(KT * NC):
                    m, (at, size) = n // NC, chunks[n % NC]
                    if n >= 4:
                        pe.wait_ge(s_x, n - 3)
                    for k in range(2 * BR):
                        if n == 0:
                            pe.wait_ge(s_n, k + 1)
                        ins = pe.matmul(z[n % 4][:, 0:size], w[:, k, m * P:(m + 1) * P], self.Y[:, k, at:at + size],
                                        start=(k == 0), stop=(k == 2 * BR - 1))
                    ins.then_inc(s_z, 1)

            @block.vector
            def _(dve):
                for br in range(2):
                    dve.wait_ge(s_sum, br + 1)
                    dve.tensor_scalar(rows[:, 0, br, 0:nt], ssum[:, 0:nt], 1.0 / ATT_W, EPS, ALU.mult, ALU.add
                                      ).then_inc(s_var, 1)
                for br in range(2):
                    dve.wait_ge(s_std, br + 1)
                    dve.reciprocal(rows[:, 2, br, 0:nt], rows[:, 1, br, 0:nt]).then_inc(s_r, 1)
                for k in range(2 * BR):
                    dve.wait_ge(s_bc, k // BR + 1)
                    dve.scalar_tensor_tensor(self.Y[:, k, 0:tok], self.Y[:, k, 0:tok],
                                             self.param("out_norm", layer * KT + k), bc[:, 0:tok], ALU.mult, ALU.mult
                                             ).then_inc(s_n, 1)
                for n in range(KT * NC):
                    m, (at, size) = n // NC, chunks[n % NC]
                    dve.wait_ge(s_z, n + 1)
                    dve.scalar_tensor_tensor(self.xT[:, m, at:at + size], z[n % 4][:, 0:size],
                                             self.mods[:, layer, 2, m, int(at >= SEQ):int(at >= SEQ) + 1],
                                             self.xT[:, m, at:at + size], ALU.mult, ALU.add).then_inc(s_x, 1)

    def feed_forward(self, layer, nt):
        self.route(layer, nt)
        self.experts(layer, nt)
        self.combine(layer, nt)

    def route(self, layer, nt):
        nc = self.nc
        NL = NG + NE
        with ExitStack() as ctx:
            hT = self.sb(ctx, "hT", [P, KT, TOK])
            hrows = self.sb(ctx, "h_rows", [P, nt, D])
            rw = self.sb(ctx, "router_w", [P, KT, NL])
            bias = self.sb(ctx, "router_b", [P, NL])
            blocks = self.sb(ctx, "block_no", [1, 64])
            lg = self.sb(ctx, "logits", [P, nt, NL])
            big = [self.sb(ctx, f"r{i}", [P, nt, NE]) for i in range(6)]
            sm = self.sb(ctx, "small", [P, 16, nt])
            g4 = self.sb(ctx, "g4", [P, 2, nt, NG])
            base = self.sb(ctx, "base", [P, nt + 1, NE])
            nb = self.sb(ctx, "blocks_of", [P, 4, NE])
            nbi = self.sb(ctx, "blocks_i", [P, 2, NE], I32)
            cmp = self.sb(ctx, "cmp", [1, 64, NE])
            blk = self.sb(ctx, "blk", [1, 2, 64])
            slotf = self.sb(ctx, "slotf", [P, 2, nt])
            bc = self.ps(ctx, "bc", [P, 3 * 512])
            ssum = self.ps(ctx, "ssum", [P, 512])
            tr = [self.ps(ctx, f"tr{i}", [P, 512]) for i in range(2)]
            pr, pcnt = self.ps(ctx, "pr", [P, 512]), self.ps(ctx, "pcnt", [P, 512])
            nrm = self.norm_open(ctx, "nf", nt)
            s_in, s_l, s_tr, s_te, s_d, s_e, s_ex, s_oh, s_cnt, s_slot, s_sc, s_tab = (
                self.sem(ctx, "r_" + n) for n in ("in", "l", "tr", "te", "d", "e", "ex", "oh", "cnt", "slot", "sc", "tab"))
            block = ctx.enter_context(nc.Block())

            @block.sync
            def _(sp):
                sp.dma_start(rw[:, :, 0:NG], self.i["router_gw"][layer].rearrange("(k p) n -> p k n", p=P)).then_inc(s_in, 16)
                sp.dma_start(rw[:, :, NG:], self.i["router_ew"][layer].rearrange("(k p) n -> p k n", p=P)).then_inc(s_in, 16)
                sp.dma_start(bias[:, 0:NG], self.i["router_gb"][layer:layer + 1, :].to_broadcast([P, NG])).then_inc(s_in, 16)
                sp.dma_start(bias[:, NG:], self.i["router_eb"][layer:layer + 1, :].to_broadcast([P, NE])).then_inc(s_in, 16)
                sp.dma_start(blocks[:], self.i["k_blocks"]).then_inc(s_in, 16)

            def exps(act):
                act.wait_ge(s_e, 1)
                act.activation(g4[:, 1, :, :], g4[:, 0, :, :], ACT.Exp)
                act.activation(sm[:, 9, :], sm[:, 8, :], ACT.Exp).then_inc(s_ex, 1)

            def counts(pe):
                pe.wait_ge(s_oh, 1)
                A = big[5][:].rearrange("p t e -> p (t e)")
                pe.matmul(pr[:, 0:nt * NE], self.c("tri"), A, start=True, stop=True)
                pe.matmul(pcnt[:, 0:nt * NE], self.c("ones"), A, start=True, stop=True).then_inc(s_cnt, 1)

            @block.scalar
            def _(act):
                self.norm_act(act, nrm, hT, layer, 1)
                for n in range(2 * nt):
                    if n == 4:
                        exps(act)
                    act.wait_ge(s_tr, n + 1)
                    act.activation(hrows[:, n // 2, (n % 2) * 512:(n % 2) * 512 + 512], tr[n % 2][:], ACT.Copy).then_inc(s_te, 1)

            @block.tensor
            def _(pe):
                self.norm_pe(pe, nrm, hT, ssum, bc)
                pe.wait_ge(s_in, 80)
                pe.wait_ge(nrm["h"], KT)
                for t in range(nt):
                    for k in range(KT):
                        ins = pe.matmul(pr[:, t * NL:(t + 1) * NL], hT[:, k, t * P:(t + 1) * P], rw[:, k, :],
                                        start=(k == 0), stop=(k == KT - 1))
                ins.then_inc(s_l, 1)
                for n in range(2 * nt):
                    if n == 8:
                        counts(pe)
                    if n >= 2:
                        pe.wait_ge(s_te, n - 1)
                    for k in range(4):
                        ins = pe.transpose(tr[n % 2][:, k * P:(k + 1) * P], hT[:, 4 * (n % 2) + k, (n // 2) * P:(n // 2 + 1) * P],
                                           self.c("ident"))
                    ins.then_inc(s_tr, 1)

            @block.vector
            def _(dve):
                self.norm_dve(dve, nrm, hT, ssum, bc)
                do = Chain(dve, s_d).step
                over_e = lambda ap: ap.unsqueeze(2).to_broadcast([P, nt, NE])
                over_g = lambda ap: ap.unsqueeze(2).to_broadcast([P, nt, NG])
                over_t = lambda ap, n=NE: ap.unsqueeze(1).to_broadcast([P, nt, n])
                dve.wait_ge(s_l, 1)
                do(dve.tensor_tensor(lg[:], pr[:, 0:nt * NL].rearrange("p (t n) -> p t n", n=NL), over_t(bias[:], NL), ALU.add))
                gl, el = lg[:, :, 0:NG], lg[:, :, NG:]
                do(dve.tensor_reduce(sm[:, 0, :], gl, AX, ALU.max))
                do(dve.tensor_tensor(g4[:, 0, :, :], gl, over_g(sm[:, 0, :]), ALU.subtract))
                do(dve.tensor_tensor(big[0][:, :, 0:NG], gl, over_g(sm[:, 0, :]), ALU.is_lt))
                do(dve.scalar_tensor_tensor(big[0][:, :, 0:NG], big[0][:, :, 0:NG], BIG, over_t(self.c("iota", NG), NG),
                                            ALU.mult, ALU.add))
                do(dve.tensor_reduce(sm[:, 1, :], big[0][:, :, 0:NG], AX, ALU.min))
                do(dve.tensor_tensor(big[0][:], over_t(self.c("group", NE)), over_e(sm[:, 1, :]), ALU.is_equal))
                do(dve.tensor_scalar(big[0][:], big[0][:], -NEG, NEG, ALU.mult, ALU.add))
                do(dve.tensor_tensor(big[0][:], el, big[0][:], ALU.add))
                for c in range(2):
                    do(dve.tensor_reduce(sm[:, 2 + c, :], big[0][:], AX, ALU.max))
                    do(dve.tensor_tensor(big[1][:], big[0][:], over_e(sm[:, 2 + c, :]), ALU.is_lt))
                    do(dve.scalar_tensor_tensor(big[1][:], big[1][:], BIG, over_t(self.c("iota", NE)), ALU.mult, ALU.add))
                    do(dve.tensor_reduce(sm[:, 4 + c, :], big[1][:], AX, ALU.min))
                    do(dve.tensor_tensor(big[2 + c][:], over_t(self.c("iota", NE)), over_e(sm[:, 4 + c, :]), ALU.is_equal))
                    if c == 0:
                        do(dve.scalar_tensor_tensor(big[0][:], big[2][:], 2 * NEG, big[0][:], ALU.mult, ALU.add))
                dve.tensor_tensor(big[5][:], big[2][:], big[3][:], ALU.add).then_inc(s_oh, 1)
                dve.tensor_tensor(sm[:, 8, :], sm[:, 3, :], sm[:, 2, :], ALU.subtract).then_inc(s_e, 1)
                dve.wait_ge(s_ex, 1)
                do(dve.tensor_reduce(sm[:, 6, :], g4[:, 1, :, :], AX, ALU.add))
                do(dve.tensor_scalar(sm[:, 10, :], sm[:, 9, :], 1.0, None, ALU.add))
                do(dve.tensor_tensor(sm[:, 10, :], sm[:, 10, :], sm[:, 6, :], ALU.mult))
                do(dve.reciprocal(self.wgt[:, 0, 0:nt], sm[:, 10, :]))
                do(dve.tensor_tensor(self.wgt[:, 1, 0:nt], self.wgt[:, 0, 0:nt], sm[:, 9, :], ALU.mult))
                dve.wait_ge(s_cnt, 1)
                do(dve.memset(base[:, 0, :], 0.0))
                for t in range(nt):
                    do(dve.tensor_tensor(base[:, t + 1, :], base[:, t, :], pcnt[:, t * NE:(t + 1) * NE], ALU.add))
                do(dve.tensor_copy(nbi[:, 0, :], base[:, nt, :]))
                do(dve.tensor_scalar(nbi[:, 0, :], nbi[:, 0, :], P - 1, None, ALU.add))
                do(dve.tensor_single_scalar(nbi[:, 1, :], nbi[:, 0, :], 7, ALU.logical_shift_right))
                do(dve.tensor_copy(nb[:, 0, :], nbi[:, 1, :]))
                do(dve.tensor_tensor_scan(nb[:, 1, :], self.c("ones", NE), nb[:, 0, :], 0.0, ALU.mult, ALU.add))
                do(dve.tensor_tensor(nb[:, 2, :], nb[:, 1, :], nb[:, 0, :], ALU.subtract))
                do(dve.scalar_tensor_tensor(base[:, 0:nt, :], over_t(nb[:, 2, :]), float(P), base[:, 0:nt, :], ALU.mult, ALU.add))
                do(dve.tensor_tensor(big[4][:], pr[:, 0:nt * NE].rearrange("p (t e) -> p t e", e=NE), base[:, 0:nt, :], ALU.add))
                for c in range(2):
                    do(dve.tensor_tensor(big[0][:], big[4][:], big[2 + c][:], ALU.mult))
                    do(dve.tensor_reduce(slotf[:, c, :], big[0][:], AX, ALU.add))
                dve.tensor_copy(self.slot[:, :, 0:nt], slotf[:]).then_inc(s_slot, 1)
                do(dve.tensor_tensor(cmp[:], nb[0:1, 1, :].unsqueeze(1).to_broadcast([1, 64, NE]),
                                     blocks[:].unsqueeze(2).to_broadcast([1, 64, NE]), ALU.is_le))
                do(dve.tensor_reduce(blk[:, 0, :], cmp[:], AX, ALU.add))
                do(dve.tensor_scalar(blk[:, 1, :], blk[:, 0, :], float(NE - 1), None, ALU.min))
                do(dve.tensor_copy(blk[:, 1, 63:64], nb[0:1, 1, NE - 1:NE]))
                do(dve.tensor_copy(self.table[:], blk[:, 1, :]))

            @block.gpsimd
            def _(pool):
                pool.wait_ge(s_slot, 1)
                for t in range(nt):
                    pool.wait_ge(s_te, 2 * t + 2)
                    for c in range(2):
                        pool.indirect_dma_start(self.xs, bass.IndirectOffsetOnAxis(self.slot[:, c, t:t + 1], 0),
                                                hrows[:, t, :], None).then_inc(s_sc, 16)
                pool.wait_ge(s_sc, 32 * nt)

    def experts(self, layer, nt):
        nc = self.nc
        STEPS = (max_blocks(nt) + 1) // 2
        W13, W2 = 4, 2
        with ExitStack() as ctx:
            w1 = self.sb(ctx, "w1", [P, 2, KT, FF])
            w3 = self.sb(ctx, "w3", [P, 2, KT, FF])
            w2 = self.sb(ctx, "w2", [P, 2, FT, D])
            xr = self.sb(ctx, "x_rows", [P, 2, D])
            xt = self.sb(ctx, "x_t", [P, 2, KT, P])
            sg = self.sb(ctx, "silu", [P, FF])
            g = self.sb(ctx, "g", [P, FF])
            gt = self.sb(ctx, "g_t", [P, FT, P])
            yr = self.sb(ctx, "y_rows", [P, 2, D])
            px = [self.ps(ctx, f"px{i}", [P, 512]) for i in range(2)]
            ph = [self.ps(ctx, f"ph{i}", [P, 512]) for i in range(2)]
            pg = [self.ps(ctx, f"pg{i}", [P, 512]) for i in range(2)]
            py = [self.ps(ctx, f"py{i}", [P, 512]) for i in range(2)]
            s_x, s_w1, s_w3, s_w2, s_st = ([self.sem(ctx, f"e_{n}{i}") for i in range(2)] for n in ("x", "w1", "w3", "w2", "st"))
            s_tx, s_xt, s_h, s_sg, s_g, s_gt, s_ge, s_y, s_ye = (
                self.sem(ctx, "e_" + n) for n in ("tx", "xt", "h", "sg", "g", "gt", "ge", "y", "ye"))
            block = ctx.enter_context(nc.Block())

            def blocks_of(eng):
                return eng.value_load(self.table[0:1, 63:64], min_val=0, max_val=max_blocks(nt))

            @block.sync
            def _(sp):
                n = blocks_of(sp)
                with sp.Fori(0, STEPS) as j:
                    for u in range(2):
                        b = 2 * j + u
                        with sp.If(b < n):
                            e = sp.value_load(self.table[0:1, bass.ds(b, 1)], min_val=0, max_val=NE - 1)
                            sp.wait_ge(s_tx, b + 1)
                            sp.dma_start(xr[:, u, :], self.xs[bass.ds(b * P, P), :]).then_inc(s_x[u], 16)
                            sp.wait_ge(s_h, 2 * b + 2)
                            for wt, name, sem in ((w1, "exp_w1", s_w1), (w3, "exp_w3", s_w3)):
                                sp.dma_start(wt[:, u, :, :],
                                             self.i[name][layer, bass.ds(e, 1), :, :].rearrange("a (k p) n -> p (a k) n", p=P)
                                             ).then_inc(sem[u], 16)
                            sp.wait_ge(s_y, b + 1)
                            sp.dma_start(w2[:, u, :, :],
                                         self.i["exp_w2"][layer, bass.ds(e, 1), :, :].rearrange("a (k p) n -> p (a k) n", p=P)
                                         ).then_inc(s_w2[u], 16)

            def transpose_x(pe, b, u, j):
                pe.wait_ge(s_x[u], 16 * j + 16)
                pe.wait_ge(s_xt, 2 * b + 2)
                for k in range(KT):
                    ins = pe.transpose(px[k // 4][:, (k % 4) * P:(k % 4 + 1) * P], xr[:, u, k * P:(k + 1) * P], self.c("ident"))
                ins.then_inc(s_tx, 1)

            @block.tensor
            def _(pe):
                n = blocks_of(pe)
                pe.sem_inc(s_tx, 2)
                pe.sem_inc(s_h, W13)
                pe.sem_inc(s_y, W2)
                transpose_x(pe, 0, 0, 0)
                with pe.Fori(0, STEPS) as j:
                    for u in range(2):
                        b = 2 * j + u
                        with pe.If(b < n):
                            pe.wait_ge(s_w1[u], 16 * j + 16)
                            pe.wait_ge(s_xt, 2 * b + 4)
                            pe.wait_ge(s_g, 2 * b)
                            for f in range(2):
                                for m, w in enumerate((w1, w3)):
                                    if f == 0 and m == 1:
                                        pe.wait_ge(s_w3[u], 16 * j + 16)
                                    for k in range(KT):
                                        ins = pe.matmul(ph[f][:, m * 256:(m + 1) * 256], xt[:, u, k, :],
                                                        w[:, u, k, f * 256:(f + 1) * 256], start=(k == 0), stop=(k == KT - 1))
                                ins.then_inc(s_h, 1)
                        with pe.If(b + 1 < n):
                            transpose_x(pe, b + 1, 1 - u, j + u)
                        with pe.If(b < n):
                            for f in range(2):
                                pe.wait_ge(s_g, 2 * b + 1 + f)
                                pe.wait_ge(s_ge, 2 * b)
                                for q in range(2):
                                    ins = pe.transpose(pg[f][:, q * P:(q + 1) * P], g[:, (2 * f + q) * P:(2 * f + q + 1) * P],
                                                       self.c("ident"))
                                ins.then_inc(s_gt, 1)
                            pe.wait_ge(s_w2[u], 16 * j + 16)
                            pe.wait_ge(s_ye, b + 1)
                            for f in range(2):
                                pe.wait_ge(s_ge, 2 * b + 1 + f)
                                for half in range(2):
                                    for q in range(2):
                                        k = 2 * f + q
                                        ins = pe.matmul(py[half][:, :], gt[:, k, :], w2[:, u, k, half * 512:(half + 1) * 512],
                                                        start=(k == 0), stop=(k == FT - 1))
                            ins.then_inc(s_y, 1)
                for u in range(2):
                    pe.wait_ge(s_st[u], ((n + 1 - u) >> 1) * 16)

            @block.scalar
            def _(act):
                n = blocks_of(act)
                act.sem_inc(s_xt, 2)
                act.sem_inc(s_ye, 1)

                def x_out(b, u):
                    act.wait_ge(s_tx, b + 3)
                    for half in range(2):
                        act.activation(xt[:, u, 4 * half:4 * half + 4, :], px[half][:, :].rearrange("p (k c) -> p k c", k=4),
                                       ACT.Copy).then_inc(s_xt, 1)

                x_out(0, 0)
                with act.Fori(0, STEPS) as j:
                    for u in range(2):
                        b = 2 * j + u
                        with act.If(b < n):
                            for f in range(2):
                                act.wait_ge(s_h, W13 + 2 * b + f + 1)
                                act.wait_ge(s_g, 2 * b)
                                act.activation(sg[:, f * 256:(f + 1) * 256], ph[f][:, 0:256], ACT.Silu
                                               ).then_inc(s_sg, 1)
                        with act.If(b + 1 < n):
                            x_out(b + 1, 1 - u)
                        with act.If(b < n):
                            act.wait_ge(s_y, W2 + b + 1)
                            act.wait_ge(s_st[u], 16 * j)
                            for half in range(2):
                                ins = act.activation(yr[:, u, half * 512:(half + 1) * 512], py[half][:, :], ACT.Copy)
                            ins.then_inc(s_ye, 1)
                            act.wait_ge(s_ye, b + 2)
                            act.dma_start(self.ys[bass.ds(b * P, P), :], yr[:, u, :]).then_inc(s_st[u], 16)

            @block.vector
            def _(dve):
                n = blocks_of(dve)
                with dve.Fori(0, STEPS) as j:
                    for u in range(2):
                        b = 2 * j + u
                        with dve.If(b < n):
                            for f in range(2):
                                dve.wait_ge(s_sg, 2 * b + f + 1)
                                dve.wait_ge(s_gt, 2 * b)
                                dve.tensor_tensor(g[:, f * 256:(f + 1) * 256], sg[:, f * 256:(f + 1) * 256],
                                                  ph[f][:, 256:512], ALU.mult).then_inc(s_g, 1)
                            for f in range(2):
                                dve.wait_ge(s_gt, 2 * b + f + 1)
                                dve.wait_ge(s_y, b + 2)
                                dve.tensor_copy(gt[:, 2 * f:2 * f + 2, :], pg[f][:, 0:2 * P].rearrange("p (q c) -> p q c", q=2)
                                                ).then_inc(s_ge, 1)

    def combine(self, layer, nt):
        nc = self.nc
        NB = 3
        with ExitStack() as ctx:
            ya = self.sb(ctx, "y_a", [P, NB, D])
            yb = self.sb(ctx, "y_b", [P, NB, D])
            pt = [self.ps(ctx, f"pt{i}", [P, 2 * 512]) for i in range(2)]
            s_ya, s_yb = ([self.sem(ctx, f"c_{n}{i}") for i in range(NB)] for n in ("ya", "yb"))
            s_wa, s_wb, s_t, s_x = (self.sem(ctx, "c_" + n) for n in ("wa", "wb", "t", "xx"))
            block = ctx.enter_context(nc.Block())

            @block.gpsimd
            def _(pool):
                for t in range(nt):
                    if t >= NB:
                        pool.wait_ge(s_t, t - NB + 1)
                    for c, (y, sem) in enumerate(((ya, s_ya), (yb, s_yb))):
                        pool.indirect_dma_start(y[:, t % NB, :], None, self.ys,
                                                bass.IndirectOffsetOnAxis(self.slot[:, c, t:t + 1], 0)).then_inc(sem[t % NB], 16)

            @block.scalar
            def _(act):
                for t in range(nt):
                    act.wait_ge(s_ya[t % NB], 16 * (t // NB + 1))
                    act.activation(ya[:, t % NB, :], ya[:, t % NB, :], ACT.Copy, scale=self.wgt[:, 0, t:t + 1]).then_inc(s_wa, 1)

            @block.vector
            def _(dve):
                for t in range(nt + 1):
                    if t < nt:
                        dve.wait_ge(s_wa, t + 1)
                        dve.wait_ge(s_yb[t % NB], 16 * (t // NB + 1))
                        dve.scalar_tensor_tensor(yb[:, t % NB, :], yb[:, t % NB, :], self.wgt[:, 1, t:t + 1], ya[:, t % NB, :],
                                                 ALU.mult, ALU.add).then_inc(s_wb, 1)
                    if t:
                        dve.wait_ge(s_t, t)
                        at = (t - 1) * P
                        for k in range(KT):
                            ins = dve.scalar_tensor_tensor(self.xT[:, k, at:at + P], pt[(t - 1) % 2][:, k * P:(k + 1) * P],
                                                           self.mods[:, layer, 5, k, int(t > LT):int(t > LT) + 1],
                                                           self.xT[:, k, at:at + P], ALU.mult, ALU.add)
                        ins.then_inc(s_x, 1)

            @block.tensor
            def _(pe):
                for t in range(nt):
                    pe.wait_ge(s_wb, t + 1)
                    if t >= 2:
                        pe.wait_ge(s_x, t - 1)
                    for k in range(KT):
                        ins = pe.transpose(pt[t % 2][:, k * P:(k + 1) * P], yb[:, t % NB, k * P:(k + 1) * P], self.c("ident"))
                    ins.then_inc(s_t, 1)

    def layer_odd(self):
        with ExitStack() as ctx:
            self.Y = self.sb(ctx, "Y", [P, 2 * BR, SEQ])
            self.odd_mixer()
            self.merge(1, LT)

    def odd_mixer(self):
        nc = self.nc
        WC = 3 * P
        GAP = LRU_ROW - 3 - CTX
        L = LRU_ROW - 3
        PAD = 8
        unit = [(i, kind, c) for i in range(BR) for kind in ("ux", "ug", "up") for c in range(3 if kind == "ux" else 2)]
        with ExitStack() as ctx:
            hT = self.sb(ctx, "hT", [P, KT, TOK])
            w = self.sb(ctx, "w_cd", [P, 2, KT, WC])
            gw = self.sb(ctx, "gate_w", [P, 2, 2, BR, P])
            pw = self.sb(ctx, "pool_weights", [P, BR, P])
            up = self.sb(ctx, "u_pad", [P, LRU_ROW])
            xl = self.sb(ctx, "x_conv", [P, L])
            lanes = [[self.sb(ctx, f"lru{d}{n}", [P, L]) for n in range(3)] for d in range(2)]
            sqr = self.sb(ctx, "a_squared", [P, L])
            pp = [self.sb(ctx, f"pool{n}", [P, PAD + SEQ + PAD]) for n in range(2)]
            z = [self.ps(ctx, f"z{i}", [P, 512]) for i in range(2)]
            pa, pxg = self.ps(ctx, "pa", [P, 3 * 512]), self.ps(ctx, "pxg", [P, 3 * 512])
            nrm = self.norm_open(ctx, "n1", NT)
            s_w = [self.sem(ctx, f"o_w{i}") for i in range(2)]
            (s_gw, s_pw, s_zero, s_z, s_ux, s_ug, s_up, s_cv, s_pg, s_r, s_a, s_q, s_sq, s_b, s_h, s_gu, s_y, s_pl, s_pd,
             s_pm, s_pe, s_ch) = (
                self.sem(ctx, "o_" + n) for n in ("gw", "pw", "zero", "z", "ux", "ug", "up", "cv", "pg", "r", "a", "q", "sqr",
                                                  "b", "h", "gu", "y", "pl", "pd", "pm", "pe", "ch"))
            block = ctx.enter_context(nc.Block())
            W = self.i["w_in_cd"][0].rearrange("(k p) n -> p k n", p=P)
            both = ((0, 0, SEQ), (SEQ, GAP, CTX))

            def wait_z_read(eng, n):
                i, kind, c = unit[n]
                if kind == "ux":
                    eng.wait_ge(s_ux, 3 * i + c + 1)
                else:
                    eng.wait_ge({"ug": s_ug, "up": s_up}[kind], 2 * i + c + 1)

            @block.sync
            def _(sp):
                sp.wait_ge(s_zero, 1)
                for d in range(2):
                    for gate, name in enumerate(("lru_wa", "lru_wx")):
                        for par in range(2):
                            sp.dma_start(gw[par * HD:(par + 1) * HD, d, gate, :, par * HD:(par + 1) * HD],
                                         self.i[name][0, d, par::2, :, :].rearrange("i h j -> h i j")).then_inc(s_gw, 16)
                sp.dma_start(pw[:], self.i["pool_w"][0].rearrange("g i j -> i g j")).then_inc(s_pw, 16)
                for i in range(BR):
                    if i >= 2:
                        sp.wait_ge(s_z, 7 * (i - 1))
                    for g, base in enumerate((0, SC_W, 2 * SC_W)):
                        sp.dma_start(w[:, i % 2, :, g * P:(g + 1) * P], W[:, :, base + i * P:base + (i + 1) * P]
                                     ).then_inc(s_w[i % 2], 16)

            @block.tensor
            def _(pe):
                self.norm_pe(pe, nrm, hT, z[0], pa)

                def gates(i, d):
                    k = 2 * i + d
                    pe.wait_ge(s_cv, i + 1)
                    if k:
                        pe.wait_ge(s_r, 2 * k)
                    for gate, ps in enumerate((pa, pxg)):
                        for at, size in CHUNKS:
                            to = at if at < SEQ else GAP
                            ins = pe.matmul(ps[:, at:at + size], gw[:, d, gate, i, :], xl[:, to:to + size],
                                            start=True, stop=True)
                    ins.then_inc(s_pg, 1)

                def pool_product(i, c, n):
                    pe.wait_ge(s_pd, i + 1)
                    wait_z_read(pe, n)
                    pe.matmul(z[n % 2][:], pw[:, i, :], pp[0][:, PAD + c * 512:PAD + (c + 1) * 512],
                              start=True, stop=True).then_inc(s_pm, 1)

                pe.wait_ge(s_gw, 16 * 8)
                pe.wait_ge(s_pw, 16)
                for n, (i, kind, c) in enumerate(unit):
                    if kind == "ux" and c == 0:
                        pe.wait_ge(s_w[i % 2], 48 * (i // 2 + 1))
                    if n >= 2:
                        wait_z_read(pe, n - 2)
                    if kind == "ug" and i:
                        pe.wait_ge(s_pe, 2 * i)
                    at, size = CHUNKS[c]
                    to = ("ux", "ug", "up").index(kind) * P
                    for k in range(KT):
                        if n == 0:
                            pe.wait_ge(nrm["h"], k + 1)
                        ins = pe.matmul(z[n % 2][:, 0:size], w[:, i % 2, k, to:to + P], hT[:, k, at:at + size],
                                        start=(k == 0), stop=(k == KT - 1))
                    ins.then_inc(s_z, 1)
                    if kind == "ug" and c == 1:
                        gates(i, 0)
                    if kind == "up" and c == 1:
                        gates(i, 1)
                    if kind == "ux" and c in (1, 2) and i:
                        pool_product(i - 1, c - 1, n)
                pool_product(BR - 1, 0, len(unit) - 2)
                pool_product(BR - 1, 1, len(unit) - 1)

            @block.scalar
            def _(act):
                self.norm_act(act, nrm, hT, 1, 0)

                def pool_out(i, c, n):
                    act.wait_ge(s_pm, 2 * i + c + 1)
                    act.activation(self.Y[:, i, c * 512:(c + 1) * 512], z[n % 2][:], ACT.Copy,
                                   scale=self.param("pool_scale", i)).then_inc(s_pe, 1)

                def gate_out(i, d):
                    k = 2 * i + d
                    R, G, S = lanes[d]
                    act.wait_ge(s_pg, k + 1)
                    if i:
                        act.wait_ge(s_y, i)
                    for gate, (dst, ps, name) in enumerate(((R, pa, "lru_ba"), (G, pxg, "lru_bx"))):
                        for at, to, size in both:
                            ins = act.activation(dst[:, to:to + size], ps[:, at:at + size], ACT.Sigmoid,
                                                 bias=self.param(name, d * BR + i))
                        ins.then_inc(s_r, 1)
                    act.wait_ge(s_r, 2 * k + 2)
                    for at, to, size in both:
                        ins = act.activation(S[:, to:to + size], R[:, to:to + size], ACT.Tanh,
                                             scale=self.decay[:, 1, d * BR + i:d * BR + i + 1])
                    ins.then_inc(s_ch, 1)
                    act.wait_ge(s_ch, k + 1)
                    for at, to, size in both:
                        ins = act.activation(R[:, to:to + size], R[:, to:to + size], ACT.Exp,
                                             scale=self.decay[:, 0, d * BR + i:d * BR + i + 1])
                    ins.then_inc(s_a, 1)

                def root(i, d):
                    k = 2 * i + d
                    S = lanes[d][2]
                    act.wait_ge(s_q, k + 1)
                    for at, to, size in both:
                        ins = act.activation(S[:, to:to + size], S[:, to:to + size], ACT.Sqrt)
                    ins.then_inc(s_sq, 1)

                for n, (i, kind, c) in enumerate(unit):
                    act.wait_ge(s_z, n + 1)
                    at, size = CHUNKS[c]
                    if kind == "ux":
                        if c == 0:
                            act.wait_ge(s_zero, 2)
                            if i:
                                act.wait_ge(s_cv, i)
                        to = 2 + at if at < SEQ else 2 + GAP
                        act.activation(up[:, to:to + size], z[n % 2][:, 0:size], ACT.Copy).then_inc(s_ux, 1)
                        if c and i:
                            pool_out(i - 1, c - 1, n)
                    elif kind == "ug":
                        act.activation(self.Y[:, BR + i, at:at + size], z[n % 2][:], ACT.Gelu_apprx_tanh).then_inc(s_ug, 1)
                        if c == 1:
                            gate_out(i, 0)
                    else:
                        if c == 0 and i:
                            act.wait_ge(s_pm, 2 * i)
                        act.activation(pp[0][:, PAD + at:PAD + at + size], z[n % 2][:], ACT.Copy).then_inc(s_up, 1)
                        if c == 1:
                            root(i, 0)
                            gate_out(i, 1)
                            root(i, 1)
                for c in range(2):
                    pool_out(BR - 1, c, len(unit) - 2 + c)

            @block.vector
            def _(dve):
                dve.memset(gw[:], 0.0).then_inc(s_zero, 1)
                for buf in (up, *pp, *(b for lane in lanes for b in lane)):
                    ins = dve.memset(buf[:], 0.0)
                ins.then_inc(s_zero, 1)
                dve.wait_ge(s_zero, 2)
                self.norm_dve(dve, nrm, hT, z[0], pa)
                link = Chain(dve, s_h)
                for i in range(BR):
                    dve.wait_ge(s_ux, 3 * i + 3)
                    if i:
                        dve.wait_ge(s_pg, 2 * i)
                        dve.wait_ge(s_gu, 2 * i)
                    link.step(dve.tensor_scalar(xl[:], up[:, 0:L], self.param("lru_conv_w", i), self.param("lru_conv_b", i),
                                                ALU.mult, ALU.add))
                    for k in (1, 2, 3):
                        ins = dve.scalar_tensor_tensor(xl[:], up[:, k:k + L], self.param("lru_conv_w", k * BR + i), xl[:],
                                                       ALU.mult, ALU.add)
                        link.step(ins)
                    dve.engine_nop().then_inc(s_cv, 1)
                    for d in range(2):
                        k = 2 * i + d
                        R, G, S = lanes[d]
                        dve.wait_ge(s_a, k + 1)
                        link.step(dve.tensor_tensor(sqr[:], R[:], R[:], ALU.mult))
                        dve.scalar_tensor_tensor(S[:], sqr[:], 1.0, S[:], ALU.add, ALU.mult).then_inc(s_q, 1)
                        dve.wait_ge(s_q, k + 1)
                        dve.wait_ge(s_gu, k + 1)
                        dve.wait_ge(s_sq, k + 1)
                        link.step(dve.tensor_tensor(S[:], S[:], G[:], ALU.mult))
                        lat, ctxs = slice(0, SEQ), slice(GAP, GAP + CTX)
                        flip = (lambda ap: ap[:, ::-1]) if d else (lambda ap: ap)
                        link.step(dve.tensor_tensor_scan(flip(G[:, ctxs]), flip(R[:, ctxs]), flip(S[:, ctxs]), 0.0,
                                                         ALU.mult, ALU.add))
                        first = G[:, GAP:GAP + 1] if d else G[:, GAP + CTX - 1:GAP + CTX]
                        link.step(dve.tensor_tensor_scan(flip(G[:, lat]), flip(R[:, lat]), flip(S[:, lat]), first,
                                                         ALU.mult, ALU.add))
                    link.step(dve.tensor_tensor(lanes[0][1][:, 0:SEQ], lanes[0][1][:, 0:SEQ], lanes[1][1][:, 0:SEQ], ALU.add))
                    dve.wait_ge(s_ug, 2 * i + 2)
                    dve.tensor_tensor(self.Y[:, BR + i, :], self.Y[:, BR + i, :], lanes[0][1][:, 0:SEQ], ALU.mult
                                      ).then_inc(s_y, 1)
                    dve.wait_ge(s_y, i + 1)

            @block.gpsimd
            def _(pool):
                n_pl = [0]

                def step(ins):
                    n_pl[0] += 1
                    ins.then_inc(s_pl, 1)
                    pool.wait_ge(s_pl, n_pl[0])

                pool.wait_ge(s_zero, 2)
                for i in range(BR):
                    for d in range(2):
                        k = 2 * i + d
                        pool.wait_ge(s_r, 2 * k + 2)
                        G = lanes[d][1]
                        pool.tensor_tensor(G[:], G[:], xl[:], ALU.mult).then_inc(s_gu, 1)
                        if d == 0:
                            pool.wait_ge(s_up, 2 * i + 2)
                            win = POOL_WINDOWS[i]
                            src, sums, size, width = pp[0], pp[1], PAD + SEQ + PAD, 1
                            while width < win:
                                size -= width
                                step(pool.tensor_tensor(sums[:, 0:size], src[:, 0:size], src[:, width:width + size], ALU.add))
                                src, width = sums, 2 * width
                            at = PAD - win // 2
                            step(pool.tensor_scalar(sums[:, 0:SEQ], sums[:, at:at + SEQ], 1.0 / win, None, ALU.mult))
                            for e, to in enumerate((0, SEQ - 8)):
                                edge = self.const[:, COL["edges"] + 16 * i + 8 * e:COL["edges"] + 16 * i + 8 * e + 8]
                                step(pool.tensor_tensor(sums[:, to:to + 8], sums[:, to:to + 8], edge, ALU.mult))
                            pool.tensor_tensor(pp[0][:, PAD:PAD + SEQ], sums[:, 0:SEQ], pp[0][:, PAD:PAD + SEQ],
                                               ALU.subtract).then_inc(s_pd, 1)

    def epilogue(self):
        nc = self.nc
        with ExitStack() as ctx:
            rows = self.sb(ctx, "out_rows", [P, 2, D])
            pt = [self.ps(ctx, f"pt{i}", [P, 2 * 512]) for i in range(2)]
            s_t, s_e = self.sem(ctx, "f_t"), self.sem(ctx, "f_e")
            s_o = [self.sem(ctx, f"f_o{i}") for i in range(2)]
            block = ctx.enter_context(nc.Block())

            @block.tensor
            def _(pe):
                for t in range(LT):
                    if t >= 2:
                        pe.wait_ge(s_e, t - 1)
                    for k in range(KT):
                        ins = pe.transpose(pt[t % 2][:, k * P:(k + 1) * P], self.xT[:, k, t * P:(t + 1) * P], self.c("ident"))
                    ins.then_inc(s_t, 1)

            @block.scalar
            def _(act):
                for t in range(LT):
                    act.wait_ge(s_t, t + 1)
                    if t >= 2:
                        act.wait_ge(s_o[t % 2], 16 * (t // 2))
                    act.activation(rows[:, t % 2, :], pt[t % 2][:, :], ACT.Copy).then_inc(s_e, 1)

            @block.sync
            def _(sp):
                for t in range(LT):
                    sp.wait_ge(s_e, t + 1)
                    sp.dma_start(self.out[0, t * P:(t + 1) * P, :], rows[:, t % 2, :]).then_inc(s_o[t % 2], 16)
                for i in range(2):
                    sp.wait_ge(s_o[i], 16 * LT // 2)


_INS = ["x", "c", "ctx", "c_ctx", "ada_w", "ada_b", "norm_mix", "norm_ffn", "out_norm", "w_out", "w_in_ab", "q_norm",
        "k_norm", "attn_sink", "sconv_w", "sconv_b", "w_in_cd", "pool_w", "pool_scale", "lru_conv_w", "lru_conv_b",
        "lru_wa", "lru_ba", "lru_wx", "lru_bx", "lru_lambda", "router_gw", "router_gb", "router_ew", "router_eb",
        "exp_w1", "exp_w3", "exp_w2"]


def build(nc, ins, out):
    Program(nc, ins, out).build()


def kernel(**inputs):
    import numpy as _np
    import concourse.bacc as _bacc
    from concourse import mybir as _mybir
    from concourse.bass_utils import run_bass_kernel_spmd as _run

    nc = _bacc.Bacc("TRN2", target_bir_lowering=False, num_devices=1)
    arrays = {f"in_{name}": _np.ascontiguousarray(inputs[name]) for name in _INS}
    arrays.update((f"in_{name}", a) for name, a in shape_constants().items())
    ins = {name[3:]: nc.dram_tensor(name, a.shape, _mybir.dt.from_np(a.dtype), kind="ExternalInput").ap()
           for name, a in arrays.items()}
    out = nc.dram_tensor("out", (1, SEQ, D), _mybir.dt.float32, kind="ExternalOutput").ap()
    build(nc, ins, out)
    return _run(nc, [arrays], core_ids=[0]).results[0]["out"]
```

```python
import numpy as np
from contextlib import ExitStack

import concourse.bass as bass
from concourse import mybir

F32 = mybir.dt.float32
F32R = mybir.dt.float32r
I32 = mybir.dt.int32
ALU = mybir.AluOpType
ACT = mybir.ActivationFunctionType
AX = mybir.AxisListType.X

P = 128
D = 1024
KT = D // P
SEQ, CTX = 1024, 256
LT, CT = SEQ // P, CTX // P
NT = LT + CT
TOK = SEQ + CTX
DEPTH = 2
N_MOD = 6
EPS = 1e-6
GRID_W = 64
HD, NQ, NKV = 64, 8, 2
QPK = NQ // NKV
KV_W = NKV * HD
ATT_W = NQ * HD
SC_W = D // 2
PAIRS = HD // 4
ROPE_BASE = 10000.0
BLK = 128
LOCAL = 3 * BLK
NEG = -1e30
BR = ATT_W // P
POOL_WINDOWS = (2, 4, 8, 16)
LRU_C = 8.0
NG, EPG = 4, 8
NE = NG * EPG
FF = D // 2
FT = FF // P
BIG = 1000.0
ADA_W = 512
ADA_UNITS = 2 * N_MOD * D // ADA_W

CHUNKS = [(0, 512), (512, 512), (1024, 256)]
SC_ROW = 1 + SEQ + 1 + 1 + CTX + 1
LRU_ROW = 2 + SEQ + 1 + 2 + CTX + 1

ROW = {}


def _rows():
    at = 0
    for name, n in (("ada_b", DEPTH * N_MOD * KT), ("norm_mix", DEPTH * KT), ("norm_ffn", DEPTH * KT),
                    ("out_norm", DEPTH * KT), ("sconv_w", 3 * BR), ("sconv_b", BR), ("pool_scale", BR),
                    ("lru_conv_w", 4 * BR), ("lru_conv_b", BR), ("lru_ba", 2 * BR), ("lru_bx", 2 * BR),
                    ("lru_lambda", 2 * BR), ("c", KT), ("c_ctx", KT), ("q_norm", 1), ("k_norm", 1)):
        ROW[name] = at
        at += n
    return at


N_ROWS = _rows()

COL = {}


def _cols():
    at = 0
    for name, n in (("ident", P), ("tri", P), ("ones", P), ("rot", P), ("headsel", 2), ("iota", NE),
                    ("group", NE), ("edges", 4 * 16)):
        COL[name] = at
        at += n
    return at


N_COLS = _cols()


def max_blocks(tiles):
    return (2 * tiles * P + NE * (P - 1)) // P


SLOTS = (max_blocks(NT) + 1) * P


def shape_constants():
    c = np.zeros((P, N_COLS), np.float32)
    i = np.arange(P)
    c[i, COL["ident"] + i] = 1
    c[:, COL["tri"]:COL["tri"] + P] = i[:, None] < i[None, :]
    c[:, COL["ones"]:COL["ones"] + P] = 1
    for base in range(0, P, 2 * PAIRS):
        for j in range(PAIRS):
            c[base + PAIRS + j, COL["rot"] + base + j] = -1
            c[base + j, COL["rot"] + base + PAIRS + j] = 1
    c[i, COL["headsel"] + i // HD] = 1
    c[:, COL["iota"]:COL["iota"] + NE] = np.arange(NE)
    c[:, COL["group"]:COL["group"] + NE] = np.arange(NE) // EPG
    for g, w in enumerate(POOL_WINDOWS):
        t = np.concatenate([np.arange(8), np.arange(SEQ - 8, SEQ)])
        n = np.clip(t + w - w // 2, 0, SEQ) - np.clip(t - w // 2, 0, SEQ)
        c[:, COL["edges"] + 16 * g:COL["edges"] + 16 * g + 16] = np.float32(w) / n.astype(np.float32)
    row, col = np.repeat(np.arange(SEQ // GRID_W), GRID_W), np.tile(np.arange(GRID_W), SEQ // GRID_W)
    freq = (np.float32(ROPE_BASE) ** (-np.arange(PAIRS, dtype=np.float32) / np.float32(PAIRS))).astype(np.float32)
    axis, pair = (i % HD) // (2 * PAIRS), i % PAIRS
    ang = np.where(axis[:, None] == 0, row[None], col[None]).astype(np.float32) * freq[pair][:, None]
    rope = np.stack([np.cos(ang), np.sin(ang)], 1).astype(np.float32)
    q, k = np.arange(BLK)[:, None], np.arange(LOCAL)[None]
    band = np.zeros((P, 3, LOCAL), np.float32)
    for m, n in enumerate((0, 1, LT - 1)):
        pos = (n - 1) * BLK + k
        ok = (np.abs(q - k + BLK) <= BLK) & (pos >= 0) & (pos < SEQ)
        band[:, m] = np.where(ok, 0, NEG)
    blocks = np.broadcast_to(np.arange(64, dtype=np.float32), (1, 64)).copy()
    return {"k_const": c, "k_rope": rope, "k_band": band, "k_blocks": blocks}


class Chain:

    def __init__(self, engine, sem):
        self.engine, self.sem, self.n = engine, sem, 0

    def step(self, ins):
        self.n += 1
        ins.then_inc(self.sem, 1)
        self.engine.wait_ge(self.sem, self.n)


class Program:
    def __init__(self, nc, ins, out):
        self.nc, self.i, self.out = nc, ins, out
        self.used = {}
        self.taken_sems = []

    def name(self, name):
        n = self.used[name] = self.used.get(name, 0) + 1
        return name if n == 1 else f"{name}_{n}"

    def sb(self, ctx, name, shape, dt=F32):
        return ctx.enter_context(self.nc.sbuf_tensor(self.name(name), shape, dt))

    def ps(self, ctx, name, shape):
        return ctx.enter_context(self.nc.psum_tensor(self.name(name), shape, F32))

    def sem(self, ctx, name):
        sem = self.nc.alloc_semaphore(self.name(name))
        self.taken_sems.append(sem)
        return sem

    def clear_semaphores(self):
        self.nc.clear_and_free_semaphores(self.taken_sems)
        self.nc.all_engine_barrier()
        self.taken_sems = []

    def c(self, name, n=None, parts=P):
        n = P if n is None else n
        return self.const[0:parts, COL[name]:COL[name] + n]

    def param(self, name, k=0):
        return self.cols[:, ROW[name] + k:ROW[name] + k + 1]

    def build(self):
        nc = self.nc
        self.xs = nc.dram_tensor("xs_slots", (SLOTS, D), F32, kind="Internal").ap()
        self.ys = self.xs
        with ExitStack() as top:
            self.const = self.sb(top, "const", [P, N_COLS])
            self.cols = self.sb(top, "cols", [P, N_ROWS])
            self.mods = self.sb(top, "mods", [P, DEPTH, N_MOD, KT, 2])
            self.gain = self.sb(top, "gain", [P, DEPTH, 2, KT, 2])
            self.decay = self.sb(top, "decay", [P, 2, 2 * BR])
            self.slot = self.sb(top, "slot", [P, 2, NT], I32)
            self.wgt = self.sb(top, "wgt", [P, 2, NT])
            self.table = self.sb(top, "table", [1, 64], I32)
            self.silu = self.sb(top, "silu_c", [P, KT, 4], F32R)
            self.xT = self.sb(top, "xT", [P, KT, TOK])
            self.prologue()
            self.layer_even()
            self.clear_semaphores()
            self.feed_forward(0, NT)
            self.clear_semaphores()
            self.layer_odd()
            self.feed_forward(1, LT)
            self.epilogue()

    def prologue(self):
        nc = self.nc
        with ExitStack() as ctx:
            rows = [self.sb(ctx, f"rows{i}", [P, P]) for i in range(2)]
            xin = self.sb(ctx, "xin", [P, 2, D])
            silu = self.sb(ctx, "silu", [P, KT, 2])
            lam = self.sb(ctx, "lam", [P, 8, 2 * BR])
            pt = [self.ps(ctx, f"pt{i}", [P, 512]) for i in range(4)]
            pr = self.ps(ctx, "pr", [P, 512])
            ada = self.ada_open(ctx, "ada0", 6)
            s_rows, s_silu, s_cols = self.sem(ctx, "s_rows"), self.sem(ctx, "s_silu"), self.sem(ctx, "s_cols")
            s_const = self.sem(ctx, "s_const")
            s_x = [self.sem(ctx, f"s_x{i}") for i in range(2)]
            s_rt, s_tp, s_te = self.sem(ctx, "s_rt"), self.sem(ctx, "s_tp"), self.sem(ctx, "s_te")
            s_dve, s_slo = self.sem(ctx, "s_dve"), self.sem(ctx, "s_slo")
            s_l, s_act = self.sem(ctx, "s_l"), self.sem(ctx, "s_act")
            block = ctx.enter_context(nc.Block())
            N_LOAD = [0]
            AHEAD = 4

            @block.scalar
            def _(act):
                act.dma_start(self.const[:], self.i["k_const"]).then_inc(s_const, 16)

                def load_rows(name, src):
                    at, n = ROW[name], src.shape[0]
                    while n:
                        take = min(n, P - at % P)
                        act.dma_start(rows[at // P][at % P:at % P + take, 0:src.shape[1]],
                                      src[0:take, :]).then_inc(s_rows, 16)
                        N_LOAD[0] += 16
                        at, n, src = at + take, n - take, src[take:, :] if n > take else None

                load_rows("ada_b", self.i["ada_b"].rearrange("l (j p) -> (l j) p", p=P))
                load_rows("norm_mix", self.i["norm_mix"].rearrange("l (j p) -> (l j) p", p=P))
                load_rows("norm_ffn", self.i["norm_ffn"].rearrange("l (j p) -> (l j) p", p=P))
                load_rows("out_norm", self.i["out_norm"].rearrange("l (j p) -> (l j) p", p=P))
                load_rows("sconv_w", self.i["sconv_w"].rearrange("a k (j p) -> (a k j) p", p=P))
                load_rows("sconv_b", self.i["sconv_b"].rearrange("a (j p) -> (a j) p", p=P))
                load_rows("pool_scale", self.i["pool_scale"].rearrange("a (j p) -> (a j) p", p=P))
                load_rows("lru_conv_w", self.i["lru_conv_w"].rearrange("a k (j p) -> (a k j) p", p=P))
                load_rows("lru_conv_b", self.i["lru_conv_b"].rearrange("a (j p) -> (a j) p", p=P))
                load_rows("lru_ba", self.i["lru_ba"].rearrange("a k (j p) -> (a k j) p", p=P))
                load_rows("lru_bx", self.i["lru_bx"].rearrange("a k (j p) -> (a k j) p", p=P))
                load_rows("lru_lambda", self.i["lru_lambda"].rearrange("a k (j p) -> (a k j) p", p=P))
                load_rows("c", self.i["c"].rearrange("a (j p) -> (a j) p", p=P))
                load_rows("c_ctx", self.i["c_ctx"].rearrange("(j p) -> j p", p=P))
                for name in ("q_norm", "k_norm"):
                    r = ROW[name]
                    for half in range(2):
                        act.dma_start(rows[r // P][r % P:r % P + 1, HD * half:HD * half + HD],
                                      self.i[name]).then_inc(s_rows, 16)
                        N_LOAD[0] += 16
                act.wait_ge(s_cols, 1)
                for k, name in enumerate(("c", "c_ctx")):
                    act.activation(silu[:, :, k], self.cols[:, ROW[name]:ROW[name] + KT], ACT.Silu).then_inc(s_silu, 1)
                act.wait_ge(s_silu, 2)
                act.activation(self.silu[:, :, 0:2], silu[:], ACT.Copy).then_inc(s_silu, 1)
                act.wait_ge(s_l, 1)
                act.activation(lam[:, 2, :], lam[:, 1, :], ACT.Exp).then_inc(s_act, 1)

                def x_out(t):
                    for half in range(2):
                        act.wait_ge(s_tp, 2 * t + half + 1)
                        act.activation(self.xT[:, 4 * half:4 * half + 4, t * P:(t + 1) * P],
                                       pt[2 * (t % 2) + half][:, :].rearrange("p (k c) -> p k c", k=4),
                                       ACT.Copy).then_inc(s_te, 1)

                for t in range(AHEAD):
                    x_out(t)
                for h in range(ADA_UNITS):
                    self.ada_act(act, ada, h)
                    if h + AHEAD < NT:
                        x_out(h + AHEAD)
                self.ada_row_out(act, ada, ADA_UNITS // 2 - 1)

            @block.sync
            def _(sp):
                def x_in(t):
                    if t >= 2:
                        sp.wait_ge(s_tp, 2 * (t - 1))
                    src = self.i["x"][0, t * P:(t + 1) * P, :] if t < LT else self.i["ctx"][0, (t - LT) * P:(t - LT + 1) * P, :]
                    sp.dma_start(xin[:, t % 2, :], src).then_inc(s_x[t % 2], 16)

                for t in range(AHEAD):
                    x_in(t)
                for h in range(ADA_UNITS):
                    self.ada_load(sp, ada, 0, h)
                    if h + AHEAD < NT:
                        x_in(h + AHEAD)

            @block.tensor
            def _(pe):
                pe.wait_ge(s_const, 16)
                pe.wait_ge(s_rows, N_LOAD[0])
                for i in range(2):
                    n = min(P, N_ROWS - i * P)
                    pe.transpose(pr[:, i * P:i * P + n], rows[i][0:n, :], self.c("ident", n, n)).then_inc(s_rt, 1)
                def x_turn(t):
                    pe.wait_ge(s_x[t % 2], 16 * (t // 2 + 1))
                    for half in range(2):
                        if t >= 2:
                            pe.wait_ge(s_te, 2 * (t - 2) + half + 1)
                        for k in range(4):
                            ins = pe.transpose(pt[2 * (t % 2) + half][:, k * P:(k + 1) * P],
                                               xin[:, t % 2, (4 * half + k) * P:(4 * half + k + 1) * P], self.c("ident"))
                        ins.then_inc(s_tp, 1)

                for t in range(AHEAD):
                    x_turn(t)
                pe.wait_ge(s_slo, 1)
                for h in range(ADA_UNITS):
                    self.ada_pe(pe, ada, h)
                    if h + AHEAD < NT:
                        x_turn(h + AHEAD)
                self.ada_turn(pe, ada, ADA_UNITS // 2 - 1)

            @block.vector
            def _(dve):
                link = Chain(dve, s_dve)
                dve.wait_ge(s_rt, 2)
                dve.tensor_copy(self.cols[:], pr[:, 0:N_ROWS]).then_inc(s_cols, 1)
                dve.wait_ge(s_cols, 1)
                dve.wait_ge(s_silu, 3)
                dve.tensor_tensor(self.silu[:, :, 2:4], silu[:], self.silu[:, :, 0:2].bitcast(F32), ALU.subtract
                                  ).then_inc(s_slo, 1)
                L = self.cols[:, ROW["lru_lambda"]:ROW["lru_lambda"] + 2 * BR]
                link.step(dve.tensor_scalar(lam[:, 0, :], L, -1.0, None, ALU.mult))
                link.step(dve.tensor_tensor(lam[:, 3, :], L, lam[:, 0, :], ALU.min))
                dve.tensor_copy(lam[:, 1, :], lam[:, 3, :]).then_inc(s_l, 1)
                dve.wait_ge(s_act, 1)
                link.step(dve.tensor_scalar(lam[:, 4, :], lam[:, 2, :], 2.0, None, ALU.add))
                link.step(dve.reciprocal(lam[:, 5, :], lam[:, 4, :]))
                link.step(dve.tensor_tensor(lam[:, 5, :], lam[:, 2, :], lam[:, 5, :], ALU.mult))
                link.step(dve.tensor_tensor(lam[:, 6, :], lam[:, 5, :], lam[:, 5, :], ALU.mult))
                link.step(dve.memset(lam[:, 7, :], 1.0 / 17))
                for n in range(7, -1, -1):
                    link.step(dve.tensor_tensor(lam[:, 7, :], lam[:, 7, :], lam[:, 6, :], ALU.mult))
                    link.step(dve.tensor_scalar(lam[:, 7, :], lam[:, 7, :], 1.0 / (2 * n + 1), None, ALU.add))
                link.step(dve.tensor_tensor(lam[:, 7, :], lam[:, 7, :], lam[:, 5, :], ALU.mult))
                link.step(dve.tensor_scalar(lam[:, 0, :], lam[:, 0, :], 0.0, None, ALU.max))
                link.step(dve.scalar_tensor_tensor(lam[:, 0, :], lam[:, 7, :], 2.0, lam[:, 0, :], ALU.mult, ALU.add))
                for s, sign in enumerate((-1.0, 1.0)):
                    link.step(dve.tensor_scalar(self.decay[:, s, :], lam[:, 0, :], sign * LRU_C, None, ALU.mult))
                link.step(dve.tensor_scalar(self.param("q_norm"), self.param("q_norm"), HD ** -0.5, None, ALU.mult))
                for h in range(ADA_UNITS):
                    self.ada_lo(dve, ada, h)
                self.ada_finish(dve, ada, 0)

    def ada_open(self, ctx, tag, nb):
        a = dict(nb=nb)
        a["raw"] = self.sb(ctx, tag + "_raw", [P, nb, KT // 2, ADA_W])
        a["hi"] = self.sb(ctx, tag + "_hi", [P, 2, KT // 2, ADA_W], F32R)
        a["lo"] = self.sb(ctx, tag + "_lo", [P, 2, KT // 2, ADA_W], F32R)
        a["row"] = self.sb(ctx, tag + "_row", [4, ADA_W])
        a["rows_ps"] = self.ps(ctx, tag + "_rows_ps", [P, 512])
        a["ps"] = self.ps(ctx, tag + "_ps", [P, 512])
        a["in"] = [self.sem(ctx, f"{tag}_in{i}") for i in range(nb)]
        for name in ("hi_done", "lo_done", "used", "row_out", "turned", "step"):
            a[name] = self.sem(ctx, f"{tag}_{name}")
        return a

    def ada_load(self, sp, a, layer, h):
        nb, n, half = a["nb"], h // 2, h % 2
        if h >= nb:
            sp.wait_ge(a["lo_done"], h - nb + 1)
        sp.dma_start(a["raw"][:, h % nb, :, :],
                     self.i["ada_w"][layer, half * (D // 2):(half + 1) * (D // 2), n * ADA_W:(n + 1) * ADA_W]
                     .rearrange("(k p) n -> p k n", p=P)).then_inc(a["in"][h % nb], 16)

    def ada_act(self, act, a, h):
        act.wait_ge(a["in"][h % a["nb"]], 16 * (h // a["nb"] + 1))
        if h >= 2:
            act.wait_ge(a["used"], h - 1)
        act.activation(a["hi"][:, h % 2, :, :], a["raw"][:, h % a["nb"], :, :], ACT.Copy).then_inc(a["hi_done"], 1)
        if h % 2 == 0 and h:
            self.ada_row_out(act, a, h // 2 - 1)

    def ada_row_out(self, act, a, n):
        act.wait_ge(a["used"], 2 * n + 2)
        act.activation(a["row"][:], a["rows_ps"][0:4, :], ACT.Copy).then_inc(a["row_out"], 1)

    def ada_lo(self, dve, a, h):
        dve.wait_ge(a["hi_done"], h + 1)
        dve.tensor_tensor(a["lo"][:, h % 2, :, :], a["raw"][:, h % a["nb"], :, :], a["hi"][:, h % 2, :, :].bitcast(F32),
                          ALU.subtract).then_inc(a["lo_done"], 1)

    def ada_turn(self, pe, a, n):
        pe.wait_ge(a["row_out"], n + 1)
        for j in range(ADA_W // P):
            at = 4 * (n * (ADA_W // P) + j)
            ins = pe.transpose(a["ps"][:, at:at + 4], a["row"][:, j * P:(j + 1) * P], self.c("ident", 4, 4))
        ins.then_inc(a["turned"], 1)

    def ada_pe(self, pe, a, h):
        n, half = h // 2, h % 2
        if h and half == 0:
            self.ada_turn(pe, a, n - 1)
        pe.wait_ge(a["lo_done"], h + 1)
        for k in range(KT // 2):
            for part in ("hi", "lo"):
                ins = pe.matmul(a["rows_ps"][0:4, :], self.silu[:, half * (KT // 2) + k, :], a[part][:, h % 2, k, :],
                                start=(half == 0 and k == 0 and part == "hi"),
                                stop=(half == 1 and k == KT // 2 - 1 and part == "lo"))
        ins.then_inc(a["used"], 1)

    def ada_finish(self, dve, a, layer):
        step = Chain(dve, a["step"]).step
        dve.wait_ge(a["turned"], ADA_UNITS // 2)
        m = self.mods[:, layer, :, :, :].rearrange("p a k s -> p (a k) s")
        b = self.cols[:, ROW["ada_b"] + layer * N_MOD * KT:ROW["ada_b"] + (layer + 1) * N_MOD * KT]
        cols = a["ps"][:, 0:4 * N_MOD * KT].rearrange("p (a s) -> p a s", s=4)
        step(dve.tensor_tensor(m, cols[:, :, 0:2], b.unsqueeze(2).to_broadcast([P, N_MOD * KT, 2]), ALU.add))
        step(dve.tensor_tensor(m, cols[:, :, 2:4], m, ALU.add))
        for w, (which, name) in enumerate(((1, "norm_mix"), (4, "norm_ffn"))):
            g = self.cols[:, ROW[name] + layer * KT:ROW[name] + (layer + 1) * KT]
            step(dve.tensor_scalar(self.gain[:, layer, w, :, :], self.mods[:, layer, which, :, :], 1.0, None, ALU.add))
            step(dve.tensor_tensor(self.gain[:, layer, w, :, :], self.gain[:, layer, w, :, :],
                                   g.unsqueeze(2).to_broadcast([P, KT, 2]), ALU.mult))

    def norm_open(self, ctx, tag, nt):
        n = dict(nt=nt, tok=nt * P)
        for name in ("sq", "acc", "sum", "var", "std", "rstd", "bc", "x", "h"):
            n[name] = self.sem(ctx, f"{tag}_{name}")
        n["rows"] = self.sb(ctx, f"{tag}_rows", [P, 4, NT])
        return n

    def norm_act(self, act, n, hT, layer, which):
        tok = n["tok"]
        for k in range(KT):
            act.activation(hT[:, k, 0:tok], self.xT[:, k, 0:tok], ACT.Square).then_inc(n["sq"], 1)
        act.wait_ge(n["var"], 1)
        act.activation(n["rows"][:, 1, 0:n["nt"]], n["rows"][:, 0, 0:n["nt"]], ACT.Sqrt).then_inc(n["std"], 1)
        for k in range(KT):
            act.wait_ge(n["x"], k + 1)
            for s, (at, m) in enumerate(((0, SEQ), (SEQ, CTX))):
                if at < tok:
                    ins = act.activation(hT[:, k, at:at + m], hT[:, k, at:at + m], ACT.Identity,
                                         bias=self.mods[:, layer, 3 * which, k, s:s + 1],
                                         scale=self.gain[:, layer, which, k, s:s + 1])
            ins.then_inc(n["h"], 1)

    def norm_pe(self, pe, n, hT, ps_sum, ps_bc):
        pe.wait_ge(n["acc"], KT - 1)
        for t in range(n["nt"]):
            ins = pe.matmul(ps_sum[:, t:t + 1], hT[:, 0, t * P:(t + 1) * P], self.c("ones", 1), start=True, stop=True)
        ins.then_inc(n["sum"], 1)
        pe.wait_ge(n["rstd"], 1)
        for t in range(n["nt"]):
            ins = pe.transpose(ps_bc[:, t * P:(t + 1) * P],
                               n["rows"][:, 3, t:t + 1].to_broadcast([P, P]), self.c("ident"))
        ins.then_inc(n["bc"], 1)

    def norm_dve(self, dve, n, hT, ps_sum, ps_bc):
        nt, tok = n["nt"], n["tok"]
        for k in range(1, KT):
            dve.wait_ge(n["sq"], k + 1)
            dve.tensor_tensor(hT[:, 0, 0:tok], hT[:, 0, 0:tok], hT[:, k, 0:tok], ALU.add).then_inc(n["acc"], 1)
            dve.wait_ge(n["acc"], k)
        dve.wait_ge(n["sum"], 1)
        dve.tensor_scalar(n["rows"][:, 0, 0:nt], ps_sum[:, 0:nt], 1.0 / D, EPS, ALU.mult, ALU.add).then_inc(n["var"], 1)
        dve.wait_ge(n["std"], 1)
        dve.reciprocal(n["rows"][:, 3, 0:nt], n["rows"][:, 1, 0:nt]).then_inc(n["rstd"], 1)
        dve.wait_ge(n["bc"], 1)
        for k in range(KT):
            dve.tensor_tensor(hT[:, k, 0:tok], self.xT[:, k, 0:tok], ps_bc[:, 0:tok], ALU.mult).then_inc(n["x"], 1)

    def layer_even(self):
        with ExitStack() as ctx:
            self.Y = self.sb(ctx, "Y", [P, 2 * BR, TOK])
            with ExitStack() as qkv:
                self.qT = self.sb(qkv, "qT", [P, BR, TOK])
                self.kT = self.sb(qkv, "kT", [P, NKV, BLK + SEQ + BLK + CTX])
                self.v = self.sb(qkv, "v_rows", [P, 1 + LT + 1 + CT, KV_W])
                self.even_projections()
                self.attention()
            self.merge(0, NT)

    def even_projections(self):
        nc = self.nc
        WC = 3 * P
        tiles = [("k", 0), ("k", 1), ("v", 0)] + [("q", i) for i in range(BR)]
        chunk_of = [(0, 0), (0, 1), (0, 2), (1, 0), (1, 1), (2, 0), (2, 1)]
        for i in range(BR):
            tiles += [("gc", i), ("gx", i), ("gb", i)]
            chunk_of += [(3 + i, 0), (3 + i, 1), (3 + i, 2)]
        NCHUNK = 3 + BR
        NC = len(CHUNKS)
        normed = [m for m, (kind, _) in enumerate(tiles) if kind in "kq"]
        K_COL = lambda at: BLK + at if at < SEQ else BLK + SEQ + BLK + at - SEQ
        with ExitStack() as ctx:
            hT = self.sb(ctx, "hT", [P, KT, TOK])
            w = self.sb(ctx, "w_ab", [P, 2, KT, WC])
            rope = self.sb(ctx, "rope", [P, 2, SEQ])
            raws, sqs = [self.Y[:, n, :] for n in (0, 1)], [self.Y[:, n, :] for n in (2, 3)]
            ta = self.sb(ctx, "ta", [P, SC_ROW])
            u = self.sb(ctx, "u", [P, SC_ROW])
            spread = tb = u[:, 0:TOK]
            hrow = self.sb(ctx, "head_rows", [P, 3, 2 * NT])
            z = [self.ps(ctx, f"z{i}", [P, 512]) for i in range(2)]
            bc = self.ps(ctx, "bc", [P, 3 * 512])
            rt = [self.ps(ctx, f"rt{i}", [P, 512]) for i in range(2)]
            ssum = self.ps(ctx, "ssum", [P, 512])
            nrm = self.norm_open(ctx, "n0", NT)
            s_w = [self.sem(ctx, f"s_w{i}") for i in range(2)]
            (s_rope, s_z, s_raw, s_rawfree, s_hs, s_hv, s_hd, s_hr, s_hb, s_n, s_rot, s_ta, s_tb, s_done,
             s_vt, s_v, s_gc, s_u, s_cv, s_y, s_pad, s_zf, s_zs, s_rc) = (
                self.sem(ctx, "s_" + n) for n in (
                    "rope", "z", "raw", "rawfree", "hs", "hv", "hd", "hr", "hb", "n", "rot", "ta", "tb", "done",
                    "vt", "v", "gc", "u", "cv", "y", "pad", "zf", "zs", "rc"))
            zero = self.sb(ctx, "zero", [P, D // 2])
            block = ctx.enter_context(nc.Block())
            W = self.i["w_in_ab"][0].rearrange("(k p) n -> p k n", p=P)
            Q0 = 2 * KV_W
            B0, C0, X0 = Q0 + ATT_W, Q0 + ATT_W + SC_W, Q0 + ATT_W + 2 * SC_W

            unit = [(m, c) for m in range(len(tiles)) for c in range(NC)]
            raw_of = {m: n for n, m in enumerate(m for m, (kind, _) in enumerate(tiles) if kind in "kqv")}

            def wait_z_read(eng, n):
                m, c = unit[n]
                kind, i = tiles[m]
                if kind in "kqv":
                    eng.wait_ge(s_raw, NC * raw_of[m] + c + 1)
                else:
                    eng.wait_ge({"gc": s_gc, "gx": s_u, "gb": s_y}[kind], NC * i + c + 1)

            arrived = []

            @block.sync
            def _(sp):
                sp.dma_start(rope[:], self.i["k_rope"]).then_inc(s_rope, 16)
                done = [0, 0]
                for ch in range(NCHUNK):
                    b = ch % 2
                    if ch >= 2:
                        last = max(m for m in range(len(tiles)) if chunk_of[m][0] == ch - 2)
                        sp.wait_ge(s_z, NC * (last + 1))
                    if ch == 0:
                        parts = [(j * P + h * HD, j * HD, HD) for j in range(2) for h in range(2)] + [(2 * P, KV_W, P)]
                    elif ch < 3:
                        parts = [(0, Q0 + (ch - 1) * 2 * P, 2 * P)]
                    else:
                        parts = [(g * P, base + (ch - 3) * P, P) for g, base in enumerate((C0, X0, B0))]
                    for to, at, n in parts:
                        sp.dma_start(w[:, b, :, to:to + n], W[:, :, at:at + n]).then_inc(s_w[b], 16)
                        done[b] += 16
                    arrived.append(done[b])

            @block.tensor
            def _(pe):
                self.norm_pe(pe, nrm, hT, ssum, bc)
                posts = []

                def head_sums(m):
                    n = normed.index(m)
                    pe.wait_ge(s_raw, NC * raw_of[m] + NC)
                    if n:
                        pe.wait_ge(s_hv, n)
                    for t in range(NT):
                        ins = pe.matmul(ssum[:, 2 * t:2 * t + 2], sqs[raw_of[m] % 2][:, t * P:(t + 1) * P], self.c("headsel", 2),
                                        start=True, stop=True)
                    ins.then_inc(s_hs, 1)

                def head_spread(m):
                    n = normed.index(m)
                    pe.wait_ge(s_hr, n + 1)
                    for t in range(NT):
                        ins = pe.transpose(bc[:, t * P:(t + 1) * P],
                                           spread[:, t * P:(t + 1) * P], self.c("ident"))
                    ins.then_inc(s_hb, 1)

                def rotate(m):
                    kind, i = tiles[m]
                    n = normed.index(m)
                    pe.wait_ge(s_n, n + 1)
                    if n:
                        pe.wait_ge(s_tb, n)
                    for c in range(2):
                        src = self.qT[:, i, c * 512:(c + 1) * 512] if kind == "q" else self.kT[:, i, BLK + c * 512:BLK + (c + 1) * 512]
                        ins = pe.matmul(rt[c][:], self.c("rot"), src, start=True, stop=True)
                    ins.then_inc(s_rot, 1)

                def v_rows(m):
                    pe.wait_ge(s_raw, NC * raw_of[m] + NC)
                    n = sum(1 for x in normed if x < m)
                    pe.wait_ge(s_n, n)
                    for t in range(NT):
                        ins = pe.transpose(bc[:, t * P:(t + 1) * P], raws[raw_of[m] % 2][:, t * P:(t + 1) * P],
                                           self.c("ident"))
                    ins.then_inc(s_vt, 1)

                for n, (m, c) in enumerate(unit):
                    if c == 0 and (m == 0 or chunk_of[m][0] != chunk_of[m - 1][0]):
                        ch = chunk_of[m][0]
                        pe.wait_ge(s_w[ch % 2], arrived[ch])
                    if n >= 2:
                        wait_z_read(pe, n - 2)
                    at, size = CHUNKS[c]
                    for k in range(KT):
                        if n == 0:
                            pe.wait_ge(nrm["h"], k + 1)
                        to = chunk_of[m][1] * P
                        ins = pe.matmul(z[n % 2][:, 0:size], w[:, chunk_of[m][0] % 2, k, to:to + P], hT[:, k, at:at + size],
                                        start=(k == 0), stop=(k == KT - 1))
                    ins.then_inc(s_z, 1)
                    if m:
                        kind = tiles[m - 1][0]
                        if kind in "kq":
                            (head_sums, head_spread, rotate)[c](m - 1)
                        elif kind == "v" and c == 0:
                            v_rows(m - 1)

            @block.scalar
            def _(act):
                self.norm_act(act, nrm, hT, 0, 0)
                sent = 0
                for n, (m, c) in enumerate(unit):
                    kind, i = tiles[m]
                    at, size = CHUNKS[c]
                    if kind in "kqv":
                        r = raw_of[m]
                        act.wait_ge(s_z, n + 1)
                        if r >= 2 and c == 0:
                            act.wait_ge(s_rawfree, r - 1)
                        raw, sq = raws[r % 2], sqs[r % 2]
                        if kind != "v":
                            act.activation(sq[:, at:at + size], z[n % 2][:, 0:size], ACT.Square)
                        act.activation(raw[:, at:at + size], z[n % 2][:, 0:size], ACT.Copy).then_inc(s_raw, 1)
                    elif kind == "gc":
                        act.wait_ge(s_z, n + 1)
                        if i:
                            act.wait_ge(s_u, NC * (i - 1) + c + 1)
                        elif c == 0:
                            act.wait_ge(s_rawfree, len(raw_of) - 1)
                        act.activation(raws[1][:, at:at + size], z[n % 2][:, 0:size], ACT.Copy).then_inc(s_gc, 1)
                    if m and c == 1 and tiles[m - 1][0] in "kq":
                        e = normed.index(m - 1)
                        act.wait_ge(s_hv, e + 1)
                        act.activation(hrow[:, 1, :], hrow[:, 0, :], ACT.Sqrt).then_inc(s_hd, 1)
                    if m and c == 1 and tiles[m - 1][0] == "v":
                        act.wait_ge(s_vt, 1)
                        act.wait_ge(s_pad, 1)
                        act.activation(self.v[:, 1:1 + LT, :], bc[:, 0:SEQ].rearrange("p (t c) -> p t c", c=P), ACT.Copy)
                        act.activation(self.v[:, 2 + LT:, :], bc[:, SEQ:TOK].rearrange("p (t c) -> p t c", c=P),
                                       ACT.Copy).then_inc(s_v, 1)

            @block.vector
            def _(dve):
                dve.memset(self.kT[:, :, 0:BLK], 0.0)
                dve.memset(self.kT[:, :, BLK + SEQ:BLK + SEQ + BLK], 0.0)
                dve.memset(self.v[:, 0, :], 0.0)
                dve.memset(self.v[:, 1 + LT, :], 0.0).then_inc(s_pad, 1)
                dve.memset(zero[:], 0.0).then_inc(s_zf, 1)
                self.norm_dve(dve, nrm, hT, ssum, bc)
                dve.wait_ge(s_rope, 16)
                link = Chain(dve, s_cv)
                for n, (m, c) in enumerate(unit):
                    kind, i = tiles[m]
                    at, size = CHUNKS[c]
                    if kind == "gx":
                        dve.wait_ge(s_gc, NC * i + c + 1)
                        dve.wait_ge(s_z, n + 1)
                        to = 1 + at if at < SEQ else 3 + at
                        dve.tensor_tensor(u[:, to:to + size], raws[1][:, at:at + size], z[n % 2][:, 0:size], ALU.mult).then_inc(s_u, 1)
                        if c == NC - 1:
                            dve.wait_ge(s_u, NC * (i + 1))
                            L = SC_ROW - 2
                            link.step(dve.tensor_scalar(ta[:, 0:L], u[:, 0:L], self.param("sconv_w", i), self.param("sconv_b", i),
                                                        ALU.mult, ALU.add))
                            for k in (1, 2):
                                link.step(dve.scalar_tensor_tensor(ta[:, 0:L], u[:, k:k + L], self.param("sconv_w", k * BR + i),
                                                                   ta[:, 0:L], ALU.mult, ALU.add))
                    elif kind == "gb":
                        dve.wait_ge(s_z, n + 1)
                        src = at if at < SEQ else 2 + at
                        dve.tensor_tensor(self.Y[:, BR + i, at:at + size], ta[:, src:src + size], z[n % 2][:, 0:size],
                                          ALU.mult).then_inc(s_y, 1)
                        if c == NC - 1:
                            dve.wait_ge(s_y, NC * (i + 1))
                    if m and tiles[m - 1][0] in "kq":
                        e = normed.index(m - 1)
                        pk, pi = tiles[m - 1]
                        raw = raws[raw_of[m - 1] % 2]
                        if c == 0:
                            dve.wait_ge(s_hs, e + 1)
                            dve.tensor_scalar(hrow[:, 0, :], ssum[:, 0:2 * NT], 1.0 / HD, EPS, ALU.mult, ALU.add).then_inc(s_hv, 1)
                        elif c == 1:
                            dve.wait_ge(s_hd, e + 1)
                            dve.reciprocal(hrow[:, 2, :], hrow[:, 1, :]).then_inc(s_rc, 1)
                            dve.wait_ge(s_rc, e + 1)
                            dve.tensor_copy(spread.rearrange("p (t c) -> p t c", c=HD),
                                            hrow[:, 2, :].unsqueeze(2).to_broadcast([P, 2 * NT, HD])).then_inc(s_hr, 1)
                            dve.wait_ge(s_hb, e + 1)
                            gain = self.param("q_norm" if pk == "q" else "k_norm")
                            if pk == "q":
                                dve.scalar_tensor_tensor(self.qT[:, pi, :], raw, gain, bc[:, 0:TOK], ALU.mult, ALU.mult
                                                         ).then_inc(s_n, 1)
                            else:
                                dve.scalar_tensor_tensor(self.kT[:, pi, BLK:BLK + SEQ], raw[:, 0:SEQ], gain, bc[:, 0:SEQ],
                                                         ALU.mult, ALU.mult)
                                dve.scalar_tensor_tensor(self.kT[:, pi, 2 * BLK + SEQ:], raw[:, SEQ:TOK], gain,
                                                         bc[:, SEQ:TOK], ALU.mult, ALU.mult).then_inc(s_n, 1)
                            dve.wait_ge(s_n, e + 1)
                            dve.engine_nop().then_inc(s_rawfree, 1)
                        else:
                            dve.wait_ge(s_rot, e + 1)
                            for h in range(2):
                                ins = dve.tensor_tensor(tb[:, h * 512:(h + 1) * 512], rt[h][:], rope[:, 1, h * 512:(h + 1) * 512],
                                                        ALU.mult)
                            ins.then_inc(s_tb, 1)
                            dve.wait_ge(s_tb, e + 1)
                            dve.wait_ge(s_ta, e + 1)
                            dst = self.qT[:, pi, 0:SEQ] if pk == "q" else self.kT[:, pi, BLK:BLK + SEQ]
                            dve.tensor_tensor(dst, ta[:, 0:SEQ], tb[:, 0:SEQ], ALU.add).then_inc(s_done, 1)
                            dve.wait_ge(s_done, e + 1)
                            if e == len(normed) - 1:
                                link.step(dve.memset(u[:], 0.0))
                    if m and c == 1 and tiles[m - 1][0] == "v":
                        dve.wait_ge(s_v, 1)
                        dve.engine_nop().then_inc(s_rawfree, 1)

            @block.gpsimd
            def _(pool):
                pool.wait_ge(s_zf, 1)
                for b in range(SLOTS // P):
                    for h in range(2):
                        pool.dma_start(self.xs[b * P:(b + 1) * P, h * D // 2:(h + 1) * D // 2], zero[:]).then_inc(s_zs, 16)
                for e, m in enumerate(normed):
                    kind, i = tiles[m]
                    pool.wait_ge(s_n, e + 1)
                    if e == 0:
                        pool.wait_ge(s_rope, 16)
                    if e:
                        pool.wait_ge(s_done, e)
                    src = self.qT[:, i, 0:SEQ] if kind == "q" else self.kT[:, i, BLK:BLK + SEQ]
                    pool.tensor_tensor(ta[:, 0:SEQ], src, rope[:, 0, :], ALU.mult).then_inc(s_ta, 1)
                pool.wait_ge(s_zs, 32 * (SLOTS // P))

    def attention(self):
        nc = self.nc
        SP_N = LOCAL + CTX
        with ExitStack() as ctx:
            band = self.sb(ctx, "band", [P, 3, LOCAL])
            sink = self.sb(ctx, "sink", [P, NQ])
            qb = self.sb(ctx, "q_block", [P, 2, BR, BLK])
            kb = self.sb(ctx, "k_block", [P, 2, NKV, LOCAL])
            S = self.sb(ctx, "scores", [P, 2, LOCAL])
            Pr = self.sb(ctx, "probs", [P, 2, SP_N])
            PT = self.sb(ctx, "probsT", [P, 2, SP_N])
            mx = self.sb(ctx, "mx", [P, 2, NQ, 4])
            den = self.sb(ctx, "den", [P, 2, NQ, 4])
            sk = self.sb(ctx, "sink_less_max", [P, NQ])
            rden = self.sb(ctx, "rden", [P, NQ])
            orow = self.sb(ctx, "o_rows", [P, ATT_W])
            pl = [self.ps(ctx, f"pl{i}", [P, 512]) for i in range(2)]
            pc = [self.ps(ctx, f"pc{i}", [P, 512]) for i in range(2)]
            ptl, ptc = self.ps(ctx, "ptl", [P, 512]), self.ps(ctx, "ptc", [P, 512])
            po, pot = self.ps(ctx, "po", [P, 512]), self.ps(ctx, "pot", [P, 512])
            (s_in, s_q, s_sc, s_m1, s_mx, s_ex, s_ptl, s_ptc, s_pel, s_pec, s_pv, s_rd, s_or, s_ot, s_y, s_snk, s_mm,
             s_dn, s_sk) = (
                self.sem(ctx, "t_" + n) for n in ("in", "q", "sc", "m1", "mx", "ex", "ptl", "ptc", "pel", "pec", "pv", "rd",
                                                  "or", "ot", "y", "snk", "mm", "dn", "sk"))
            block = ctx.enter_context(nc.Block())

            def wait(eng, sem, count):
                if not isinstance(count, int) or count > 0:
                    eng.wait_ge(sem, count)

            def behind(n, h, k):
                return (n, h - k) if h >= k else (n - 1, h - k + NQ)

            def over_blocks(eng, one_block):
                one_block(0, 0, True, None, 0)
                with eng.Fori(0, (LT - 2) // 2) as j:
                    one_block(2 * j + 1, 1, True, True, 1)
                    one_block(2 * j + 2, 0, True, True, 1)
                one_block(LT - 1, 1, True, True, 2)
                for n in range(LT, NT):
                    one_block(n, n % 2, False, n == LT, None)

            @block.sync
            def _(sp):
                sp.dma_start(band[:], self.i["k_band"]).then_inc(s_in, 16)
                sp.dma_start(sink[:], self.i["attn_sink"].to_broadcast([P, NQ])).then_inc(s_in, 16)

            @block.gpsimd
            def _(pool):
                def lay_out(n, par, local):
                    wait(pool, s_sc, (n - 1) * NQ)
                    if local:
                        pool.tensor_copy(kb[:, par, :, :], self.kT[:, :, bass.ds(n * BLK, LOCAL)])
                    pool.tensor_copy(qb[:, par, :, :], self.qT[:, :, bass.ds(n * BLK, BLK)]).then_inc(s_q, 1)

                lay_out(0, 0, True)
                lay_out(1, 1, True)
                with pool.Fori(0, (LT - 2) // 2) as j:
                    lay_out(2 * j + 2, 0, True)
                    lay_out(2 * j + 3, 1, True)
                for n in range(LT, NT):
                    lay_out(n, n % 2, False)

            @block.tensor
            def _(pe):
                def scores(n, par, h, local):
                    g, t, lo = h // QPK, h // 2, h % 2 * HD
                    u, hi = n * NQ + h, lo + HD
                    wait(pe, s_ex, u - 1)
                    if local:
                        pe.matmul(pl[h % 2][:, 0:LOCAL], qb[lo:hi, par, t, :], kb[lo:hi, par, g, :], start=True, stop=True)
                    pe.matmul(pc[h % 2][:, 0:CTX], qb[lo:hi, par, t, :], self.kT[lo:hi, g, 2 * BLK + SEQ:],
                              start=True, stop=True).then_inc(s_sc, 1)

                def products(n, h, local):
                    u, b, g = n * NQ + h, h % 2, h // QPK
                    out = po[:, h * HD:(h + 1) * HD]
                    if h == 0:
                        wait(pe, s_or, n)
                    if local:
                        pe.wait_ge(s_pel, u + 1)
                        for j in range(3):
                            pe.matmul(out, PT[:, b, j * P:(j + 1) * P],
                                      self.v[:, bass.ds(n + j, 1), g * HD:(g + 1) * HD].squeeze(1) if not isinstance(n, int)
                                      else self.v[:, n + j, g * HD:(g + 1) * HD], start=(j == 0), stop=False)
                    pe.wait_ge(s_pec, u + 1)
                    for j in range(CT):
                        ins = pe.matmul(out, PT[:, b, LOCAL + j * P:LOCAL + (j + 1) * P],
                                        self.v[:, 2 + LT + j, g * HD:(g + 1) * HD],
                                        start=(not local and j == 0), stop=(j == CT - 1))
                    ins.then_inc(s_pv, 1)

                def transposes(n, h, local):
                    u, b = n * NQ + h, h % 2
                    pe.wait_ge(s_ex, u + 1)
                    if local:
                        wait(pe, s_pel, u)
                        for j in range(3):
                            ins = pe.transpose(ptl[:, j * P:(j + 1) * P], Pr[:, b, j * P:(j + 1) * P], self.c("ident"))
                        ins.then_inc(s_ptl, 1)
                    wait(pe, s_pec, u)
                    for j in range(CT):
                        ins = pe.transpose(ptc[:, j * P:(j + 1) * P], Pr[:, b, LOCAL + j * P:LOCAL + (j + 1) * P],
                                           self.c("ident"))
                    ins.then_inc(s_ptc, 1)

                def output(n):
                    pe.wait_ge(s_or, n + 1)
                    for j in range(BR):
                        ins = pe.transpose(pot[:, j * P:(j + 1) * P], orow[:, j * P:(j + 1) * P], self.c("ident"))
                    ins.then_inc(s_ot, 1)

                def one_block(n, par, local, before, _):
                    pe.wait_ge(s_q, n + 1)
                    for h in range(NQ):
                        scores(n, par, h, local)
                        for k, work in ((2, products), (1, transposes)):
                            if h >= k or before is not None:
                                work(*behind(n, h, k), local if h >= k else before)
                        if h == 3 and before is not None:
                            output(n - 1)

                over_blocks(pe, one_block)
                products(NT - 1, NQ - 2, False)
                transposes(NT - 1, NQ - 1, False)
                products(NT - 1, NQ - 1, False)
                output(NT - 1)

            @block.vector
            def _(dve):
                def maxima(n, par, h, local, m):
                    u, b = n * NQ + h, h % 2
                    dve.wait_ge(s_sc, u + 1)
                    wait(dve, s_ex, u - 1)
                    ins = dve.reduce_max(mx[:, par, h, 1:2], pc[b][:, 0:CTX], AX)
                    if local:
                        ins = dve.tensor_tensor_reduce(out=S[:, b, :], in0=pl[b][:, 0:LOCAL], in1=band[:, m, :], scale=1.0,
                                                       scalar=sink[:, h:h + 1], op0=ALU.add, op1=ALU.max,
                                                       accum_out=mx[:, par, h, 0:1])
                    ins.then_inc(s_m1, 1)
                    dve.wait_ge(s_m1, u + 1)
                    dve.tensor_scalar(mx[:, par, h, 3:4], mx[:, par, h, 0:1] if local else sink[:, h:h + 1],
                                      mx[:, par, h, 1:2], -1.0, ALU.max, ALU.mult).then_inc(s_mx, 1)

                def copy_out(n, h):
                    u, b = n * NQ + h, h % 2
                    dve.wait_ge(s_ptl, u + 1)
                    wait(dve, s_pv, u - 1)
                    dve.tensor_copy(PT[:, b, 0:LOCAL], ptl[:, 0:LOCAL]).then_inc(s_pel, 1)

                def rows_out(n, par, local):
                    dve.wait_ge(s_snk, n + 1)
                    dve.tensor_reduce(den[:, par, :, 3], den[:, par, :, (0 if local else 1):3], AX, ALU.add).then_inc(s_dn, 1)
                    dve.wait_ge(s_dn, n + 1)
                    dve.reciprocal(rden[:], den[:, par, :, 3]).then_inc(s_rd, 1)
                    dve.wait_ge(s_rd, n + 1)
                    dve.wait_ge(s_pv, n * NQ + NQ)
                    dve.tensor_tensor(orow[:].rearrange("p (h c) -> p h c", h=NQ), po[:, :].rearrange("p (h c) -> p h c", h=NQ),
                                      rden[:].unsqueeze(2).to_broadcast([P, NQ, HD]), ALU.mult).then_inc(s_or, 1)

                def one_block(n, par, local, before, m):
                    for h in range(NQ):
                        maxima(n, par, h, local, m)
                        if h == NQ - 1:
                            dve.wait_ge(s_mx, n * NQ + NQ)
                            dve.tensor_tensor(sk[:], sink[:], mx[:, par, :, 3], ALU.add).then_inc(s_sk, 1)
                        if h == 1 and before is not None:
                            rows_out(n - 1, 1 - par, before)
                        if local if h else before:
                            copy_out(*behind(n, h, 1))

                dve.wait_ge(s_in, 32)
                over_blocks(dve, one_block)
                rows_out(NT - 1, (NT - 1) % 2, False)

            @block.scalar
            def _(act):
                def exponentials(n, par, h, local):
                    u, b = n * NQ + h, h % 2
                    act.wait_ge(s_mx, u + 1)
                    wait(act, s_ptc, u - 1)
                    if local:
                        act.activation(Pr[:, b, 0:LOCAL], S[:, b, :], ACT.Exp, bias=mx[:, par, h, 3:4],
                                       accum_out=den[:, par, h, 0:1])
                    act.activation(Pr[:, b, LOCAL:], pc[b][:, 0:CTX], ACT.Exp, bias=mx[:, par, h, 3:4],
                                   accum_out=den[:, par, h, 1:2]).then_inc(s_ex, 1)

                def copy_out(n, h):
                    u, b = n * NQ + h, h % 2
                    act.wait_ge(s_ptc, u + 1)
                    wait(act, s_pv, u - 1)
                    act.activation(PT[:, b, LOCAL:], ptc[:, 0:CTX], ACT.Copy).then_inc(s_pec, 1)

                def output(n):
                    act.wait_ge(s_ot, n + 1)
                    act.activation(self.Y[:, 0:BR, bass.ds(n * BLK, BLK)], pot[:, :].rearrange("p (j c) -> p j c", j=BR),
                                   ACT.Copy).then_inc(s_y, 1)

                def one_block(n, par, local, before, _):
                    for h in range(NQ):
                        exponentials(n, par, h, local)
                        if h == NQ - 1:
                            act.wait_ge(s_sk, n + 1)
                            act.activation(den[:, par, :, 2], sk[:], ACT.Exp).then_inc(s_snk, 1)
                        if h or before is not None:
                            copy_out(*behind(n, h, 1))
                        if h == 3 and before is not None:
                            output(n - 1)

                act.wait_ge(s_in, 32)
                over_blocks(act, one_block)
                copy_out(NT - 1, NQ - 1)
                output(NT - 1)

    def merge(self, layer, nt):
        nc = self.nc
        tok = nt * P
        chunks = [(a, n) for a, n in CHUNKS if a < tok]
        NC = len(chunks)
        with ExitStack() as ctx:
            w = self.sb(ctx, "w_o", [P, 2 * BR, D])
            sq = self.sb(ctx, "sq", [P, 2 * BR, tok])
            rows = self.sb(ctx, "rows", [P, 3, 2, NT])
            bc = self.ps(ctx, "bc", [P, 3 * 512])
            z = [self.ps(ctx, f"z{i}", [P, 512]) for i in range(2)]
            ssum = self.ps(ctx, "ssum", [P, 512])
            ada = self.ada_open(ctx, "ada1", 2) if layer + 1 < DEPTH else None
            s_w, s_sq, s_acc, s_sum, s_var, s_std, s_r, s_bc, s_n, s_z, s_x = (
                self.sem(ctx, "m_" + n) for n in ("w", "sq", "acc", "sum", "var", "std", "r", "bc", "n", "z", "x"))
            block = ctx.enter_context(nc.Block())

            @block.sync
            def _(sp):
                for k in range(2):
                    sp.dma_start(w[:, :, k * 512:(k + 1) * 512],
                                 self.i["w_out"][layer, :, k * 512:(k + 1) * 512].rearrange("(k p) n -> p k n", p=P)
                                 ).then_inc(s_w, 16)
                if ada:
                    for h in range(ADA_UNITS):
                        self.ada_load(sp, ada, layer + 1, h)

            @block.scalar
            def _(act):
                for k in range(2 * BR):
                    act.activation(sq[:, k, :], self.Y[:, k, 0:tok], ACT.Square).then_inc(s_sq, 1)
                for br in range(2):
                    act.wait_ge(s_var, br + 1)
                    act.activation(rows[:, 1, br, 0:nt], rows[:, 0, br, 0:nt], ACT.Sqrt).then_inc(s_std, 1)
                if ada:
                    for h in range(ADA_UNITS):
                        self.ada_act(act, ada, h)
                    self.ada_row_out(act, ada, ADA_UNITS // 2 - 1)

            @block.tensor
            def _(pe):
                for br in range(2):
                    if br:
                        pe.wait_ge(s_var, 1)
                    pe.wait_ge(s_acc, (br + 1) * (BR - 1))
                    for t in range(nt):
                        ins = pe.matmul(ssum[:, t:t + 1], sq[:, br * BR, t * P:(t + 1) * P], self.c("ones", 1),
                                        start=True, stop=True)
                    ins.then_inc(s_sum, 1)
                for br in range(2):
                    pe.wait_ge(s_r, br + 1)
                    if br:
                        pe.wait_ge(s_n, BR)
                    for t in range(nt):
                        ins = pe.transpose(bc[:, t * P:(t + 1) * P], rows[:, 2, br, t:t + 1].to_broadcast([P, P]),
                                           self.c("ident"))
                    ins.then_inc(s_bc, 1)
                pe.wait_ge(s_w, 32)
                for n in range(KT * NC):
                    m, (at, size) = n // NC, chunks[n % NC]
                    if n >= 2:
                        pe.wait_ge(s_x, n - 1)
                    for k in range(2 * BR):
                        if n == 0:
                            pe.wait_ge(s_n, k + 1)
                        ins = pe.matmul(z[n % 2][:, 0:size], w[:, k, m * P:(m + 1) * P], self.Y[:, k, at:at + size],
                                        start=(k == 0), stop=(k == 2 * BR - 1))
                    ins.then_inc(s_z, 1)
                    if ada:
                        self.ada_pe(pe, ada, n)
                if ada:
                    self.ada_turn(pe, ada, ADA_UNITS // 2 - 1)

            @block.vector
            def _(dve):
                for br in range(2):
                    for k in range(1, BR):
                        total = sq[:, br * BR, :]
                        dve.wait_ge(s_sq, br * BR + k + 1)
                        dve.tensor_tensor(total, total, sq[:, br * BR + k, :], ALU.add).then_inc(s_acc, 1)
                        dve.wait_ge(s_acc, br * (BR - 1) + k)
                for br in range(2):
                    dve.wait_ge(s_sum, br + 1)
                    dve.tensor_scalar(rows[:, 0, br, 0:nt], ssum[:, 0:nt], 1.0 / ATT_W, EPS, ALU.mult, ALU.add
                                      ).then_inc(s_var, 1)
                for br in range(2):
                    dve.wait_ge(s_std, br + 1)
                    dve.reciprocal(rows[:, 2, br, 0:nt], rows[:, 1, br, 0:nt]).then_inc(s_r, 1)
                for k in range(2 * BR):
                    dve.wait_ge(s_bc, k // BR + 1)
                    dve.scalar_tensor_tensor(self.Y[:, k, 0:tok], self.Y[:, k, 0:tok],
                                             self.param("out_norm", layer * KT + k), bc[:, 0:tok], ALU.mult, ALU.mult
                                             ).then_inc(s_n, 1)
                for n in range(KT * NC):
                    m, (at, size) = n // NC, chunks[n % NC]
                    if ada:
                        self.ada_lo(dve, ada, n)
                    dve.wait_ge(s_z, n + 1)
                    dve.scalar_tensor_tensor(self.xT[:, m, at:at + size], z[n % 2][:, 0:size],
                                             self.mods[:, layer, 2, m, int(at >= SEQ):int(at >= SEQ) + 1],
                                             self.xT[:, m, at:at + size], ALU.mult, ALU.add).then_inc(s_x, 1)
                if ada:
                    self.ada_finish(dve, ada, layer + 1)

    def feed_forward(self, layer, nt):
        self.route(layer, nt)
        self.experts(layer, nt)
        self.combine(layer, nt)

    def route(self, layer, nt):
        nc = self.nc
        NL = NG + NE
        with ExitStack() as ctx:
            hT = self.sb(ctx, "hT", [P, KT, TOK])
            hrows = self.sb(ctx, "h_rows", [P, nt, D])
            rw = self.sb(ctx, "router_w", [P, KT, NL])
            bias = self.sb(ctx, "router_b", [P, NL])
            blocks = self.sb(ctx, "block_no", [1, 64])
            lg = self.sb(ctx, "logits", [P, nt, NL])
            big = [self.sb(ctx, f"r{i}", [P, nt, NE]) for i in range(6)]
            sm = self.sb(ctx, "small", [P, 16, nt])
            g4 = self.sb(ctx, "g4", [P, 2, nt, NG])
            base = self.sb(ctx, "base", [P, nt + 1, NE])
            nb = self.sb(ctx, "blocks_of", [P, 4, NE])
            nbi = self.sb(ctx, "blocks_i", [P, 2, NE], I32)
            cmp = self.sb(ctx, "cmp", [1, 64, NE])
            blk = self.sb(ctx, "blk", [1, 2, 64])
            slotf = self.sb(ctx, "slotf", [P, 2, nt])
            bc = self.ps(ctx, "bc", [P, 3 * 512])
            ssum = self.ps(ctx, "ssum", [P, 512])
            tr = [self.ps(ctx, f"tr{i}", [P, 512]) for i in range(2)]
            pr, pcnt = self.ps(ctx, "pr", [P, 512]), self.ps(ctx, "pcnt", [P, 512])
            nrm = self.norm_open(ctx, "nf", nt)
            s_in, s_l, s_tr, s_te, s_d, s_e, s_ex, s_oh, s_cnt, s_slot, s_sc, s_tab = (
                self.sem(ctx, "r_" + n) for n in ("in", "l", "tr", "te", "d", "e", "ex", "oh", "cnt", "slot", "sc", "tab"))
            block = ctx.enter_context(nc.Block())

            @block.sync
            def _(sp):
                sp.dma_start(rw[:, :, 0:NG], self.i["router_gw"][layer].rearrange("(k p) n -> p k n", p=P)).then_inc(s_in, 16)
                sp.dma_start(rw[:, :, NG:], self.i["router_ew"][layer].rearrange("(k p) n -> p k n", p=P)).then_inc(s_in, 16)
                sp.dma_start(bias[:, 0:NG], self.i["router_gb"][layer:layer + 1, :].to_broadcast([P, NG])).then_inc(s_in, 16)
                sp.dma_start(bias[:, NG:], self.i["router_eb"][layer:layer + 1, :].to_broadcast([P, NE])).then_inc(s_in, 16)
                sp.dma_start(blocks[:], self.i["k_blocks"]).then_inc(s_in, 16)

            def exps(act):
                act.wait_ge(s_e, 1)
                act.activation(g4[:, 1, :, :], g4[:, 0, :, :], ACT.Exp)
                act.activation(sm[:, 9, :], sm[:, 8, :], ACT.Exp).then_inc(s_ex, 1)

            def counts(pe):
                pe.wait_ge(s_oh, 1)
                A = big[5][:].rearrange("p t e -> p (t e)")
                pe.matmul(pr[:, 0:nt * NE], self.c("tri"), A, start=True, stop=True)
                pe.matmul(pcnt[:, 0:nt * NE], self.c("ones"), A, start=True, stop=True).then_inc(s_cnt, 1)

            @block.scalar
            def _(act):
                self.norm_act(act, nrm, hT, layer, 1)
                for n in range(2 * nt):
                    if n == 4:
                        exps(act)
                    act.wait_ge(s_tr, n + 1)
                    act.activation(hrows[:, n // 2, (n % 2) * 512:(n % 2) * 512 + 512], tr[n % 2][:], ACT.Copy).then_inc(s_te, 1)

            @block.tensor
            def _(pe):
                self.norm_pe(pe, nrm, hT, ssum, bc)
                pe.wait_ge(s_in, 80)
                pe.wait_ge(nrm["h"], KT)
                for t in range(nt):
                    for k in range(KT):
                        ins = pe.matmul(pr[:, t * NL:(t + 1) * NL], hT[:, k, t * P:(t + 1) * P], rw[:, k, :],
                                        start=(k == 0), stop=(k == KT - 1))
                ins.then_inc(s_l, 1)
                for n in range(2 * nt):
                    if n == 8:
                        counts(pe)
                    if n >= 2:
                        pe.wait_ge(s_te, n - 1)
                    for k in range(4):
                        ins = pe.transpose(tr[n % 2][:, k * P:(k + 1) * P], hT[:, 4 * (n % 2) + k, (n // 2) * P:(n // 2 + 1) * P],
                                           self.c("ident"))
                    ins.then_inc(s_tr, 1)

            @block.vector
            def _(dve):
                self.norm_dve(dve, nrm, hT, ssum, bc)
                do = Chain(dve, s_d).step
                over_e = lambda ap: ap.unsqueeze(2).to_broadcast([P, nt, NE])
                over_g = lambda ap: ap.unsqueeze(2).to_broadcast([P, nt, NG])
                over_t = lambda ap, n=NE: ap.unsqueeze(1).to_broadcast([P, nt, n])
                dve.wait_ge(s_l, 1)
                do(dve.tensor_tensor(lg[:], pr[:, 0:nt * NL].rearrange("p (t n) -> p t n", n=NL), over_t(bias[:], NL), ALU.add))
                gl, el = lg[:, :, 0:NG], lg[:, :, NG:]
                do(dve.tensor_reduce(sm[:, 0, :], gl, AX, ALU.max))
                do(dve.tensor_tensor(g4[:, 0, :, :], gl, over_g(sm[:, 0, :]), ALU.subtract))
                do(dve.tensor_tensor(big[0][:, :, 0:NG], gl, over_g(sm[:, 0, :]), ALU.is_lt))
                do(dve.scalar_tensor_tensor(big[0][:, :, 0:NG], big[0][:, :, 0:NG], BIG, over_t(self.c("iota", NG), NG),
                                            ALU.mult, ALU.add))
                do(dve.tensor_reduce(sm[:, 1, :], big[0][:, :, 0:NG], AX, ALU.min))
                do(dve.tensor_tensor(big[0][:], over_t(self.c("group", NE)), over_e(sm[:, 1, :]), ALU.is_equal))
                do(dve.tensor_scalar(big[0][:], big[0][:], -NEG, NEG, ALU.mult, ALU.add))
                do(dve.tensor_tensor(big[0][:], el, big[0][:], ALU.add))
                for c in range(2):
                    do(dve.tensor_reduce(sm[:, 2 + c, :], big[0][:], AX, ALU.max))
                    do(dve.tensor_tensor(big[1][:], big[0][:], over_e(sm[:, 2 + c, :]), ALU.is_lt))
                    do(dve.scalar_tensor_tensor(big[1][:], big[1][:], BIG, over_t(self.c("iota", NE)), ALU.mult, ALU.add))
                    do(dve.tensor_reduce(sm[:, 4 + c, :], big[1][:], AX, ALU.min))
                    do(dve.tensor_tensor(big[2 + c][:], over_t(self.c("iota", NE)), over_e(sm[:, 4 + c, :]), ALU.is_equal))
                    if c == 0:
                        do(dve.scalar_tensor_tensor(big[0][:], big[2][:], 2 * NEG, big[0][:], ALU.mult, ALU.add))
                dve.tensor_tensor(big[5][:], big[2][:], big[3][:], ALU.add).then_inc(s_oh, 1)
                dve.tensor_tensor(sm[:, 8, :], sm[:, 3, :], sm[:, 2, :], ALU.subtract).then_inc(s_e, 1)
                dve.wait_ge(s_ex, 1)
                do(dve.tensor_reduce(sm[:, 6, :], g4[:, 1, :, :], AX, ALU.add))
                do(dve.tensor_scalar(sm[:, 10, :], sm[:, 9, :], 1.0, None, ALU.add))
                do(dve.tensor_tensor(sm[:, 10, :], sm[:, 10, :], sm[:, 6, :], ALU.mult))
                do(dve.reciprocal(self.wgt[:, 0, 0:nt], sm[:, 10, :]))
                do(dve.tensor_tensor(self.wgt[:, 1, 0:nt], self.wgt[:, 0, 0:nt], sm[:, 9, :], ALU.mult))
                dve.wait_ge(s_cnt, 1)
                do(dve.memset(base[:, 0, :], 0.0))
                for t in range(nt):
                    do(dve.tensor_tensor(base[:, t + 1, :], base[:, t, :], pcnt[:, t * NE:(t + 1) * NE], ALU.add))
                do(dve.tensor_copy(nbi[:, 0, :], base[:, nt, :]))
                do(dve.tensor_scalar(nbi[:, 0, :], nbi[:, 0, :], P - 1, None, ALU.add))
                do(dve.tensor_single_scalar(nbi[:, 1, :], nbi[:, 0, :], 7, ALU.logical_shift_right))
                do(dve.tensor_copy(nb[:, 0, :], nbi[:, 1, :]))
                do(dve.tensor_tensor_scan(nb[:, 1, :], self.c("ones", NE), nb[:, 0, :], 0.0, ALU.mult, ALU.add))
                do(dve.tensor_tensor(nb[:, 2, :], nb[:, 1, :], nb[:, 0, :], ALU.subtract))
                do(dve.scalar_tensor_tensor(base[:, 0:nt, :], over_t(nb[:, 2, :]), float(P), base[:, 0:nt, :], ALU.mult, ALU.add))
                do(dve.tensor_tensor(big[4][:], pr[:, 0:nt * NE].rearrange("p (t e) -> p t e", e=NE), base[:, 0:nt, :], ALU.add))
                for c in range(2):
                    do(dve.tensor_tensor(big[0][:], big[4][:], big[2 + c][:], ALU.mult))
                    do(dve.tensor_reduce(slotf[:, c, :], big[0][:], AX, ALU.add))
                dve.tensor_copy(self.slot[:, :, 0:nt], slotf[:]).then_inc(s_slot, 1)
                do(dve.tensor_tensor(cmp[:], nb[0:1, 1, :].unsqueeze(1).to_broadcast([1, 64, NE]),
                                     blocks[:].unsqueeze(2).to_broadcast([1, 64, NE]), ALU.is_le))
                do(dve.tensor_reduce(blk[:, 0, :], cmp[:], AX, ALU.add))
                do(dve.tensor_scalar(blk[:, 1, :], blk[:, 0, :], float(NE - 1), None, ALU.min))
                do(dve.tensor_copy(blk[:, 1, 63:64], nb[0:1, 1, NE - 1:NE]))
                do(dve.tensor_scalar(blk[:, 1, 62:63], nb[0:1, 1, NE - 1:NE], -1.0, None, ALU.add))
                do(dve.tensor_copy(self.table[:], blk[:, 1, :]))
                do(dve.tensor_single_scalar(self.table[:, 62:63], self.table[:, 62:63], 1, ALU.logical_shift_right))

            @block.gpsimd
            def _(pool):
                pool.wait_ge(s_slot, 1)
                for t in range(nt):
                    pool.wait_ge(s_te, 2 * t + 2)
                    for c in range(2):
                        pool.indirect_dma_start(self.xs, bass.IndirectOffsetOnAxis(self.slot[:, c, t:t + 1], 0),
                                                hrows[:, t, :], None).then_inc(s_sc, 16)
                pool.wait_ge(s_sc, 32 * nt)

    def experts(self, layer, nt):
        nc = self.nc
        STEPS = (max_blocks(nt) + 1) // 2
        NC = 6
        HK = KT // 2
        RING = 4
        with ExitStack() as ctx:
            w = self.sb(ctx, "w_raw", [P, NC, HK * FF])
            wh = self.sb(ctx, "w_hi", [P, RING, HK * FF], F32R)
            wl = self.sb(ctx, "w_lo", [P, RING, HK * FF], F32R)
            xr = self.sb(ctx, "x_rows", [P, 2, D])
            xh = self.sb(ctx, "x_t_hi", [P, 2, D], F32R)
            xl = self.sb(ctx, "x_t_lo", [P, 2, D], F32R)
            sg = self.sb(ctx, "silu", [P, FF])
            g = self.sb(ctx, "g", [P, FF])
            gh = self.sb(ctx, "g_t_hi", [P, FF], F32R)
            gl = self.sb(ctx, "g_t_lo", [P, FF], F32R)
            yr = self.sb(ctx, "y_rows", [P, D])
            px, pg = self.ps(ctx, "px", [P, 512]), self.ps(ctx, "pg", [P, 512])
            ph = [[self.ps(ctx, f"ph{u}{m}", [P, 512]) for m in range(2)] for u in range(2)]
            py = [self.ps(ctx, f"py{i}", [P, 512]) for i in range(2)]
            s_x = [self.sem(ctx, f"e_x{i}") for i in range(2)]
            s_w, s_hi, s_lo, s_c = ([self.sem(ctx, f"e_{n}{c}") for c in range(NC)] for n in ("w", "hi", "lo", "c"))
            s_tx, s_xh, s_xl, s_sg, s_g, s_gt, s_gh, s_gl, s_ye, s_st = (
                self.sem(ctx, "e_" + n) for n in ("tx", "xh", "xl", "sg", "g", "gt", "gh", "gl", "ye", "st"))
            block = ctx.enter_context(nc.Block())

            def over_blocks(eng, body):
                n = eng.value_load(self.table[0:1, 63:64], min_val=2, max_val=max_blocks(nt))
                with eng.Fori(0, STEPS - 1) as j:
                    with eng.If(2 * j + 2 < n):
                        body(j, 0, 2)
                        body(j, 1, 2)
                last = eng.value_load(self.table[0:1, 62:63], min_val=0, max_val=STEPS - 1)
                body(last, 0, 1)
                body(last, 1, 0)
                return last

            def slot(c, parity):
                return (parity * NC + c) % RING

            def block_of(c, cycle):
                return cycle if c in (2, 3) else cycle + 1

            @block.sync
            def _(sp):
                def rows(m, u):
                    sp.dma_start(xr[:, u, :], self.xs[bass.ds(m * P, P), :]).then_inc(s_x[u], 16)

                def weights(m, chunks, used):
                    e = sp.value_load(self.table[0:1, bass.ds(m, 1)], min_val=0, max_val=NE - 1)

                    def load():
                        for c in chunks:
                            if used is not None:
                                sp.wait_ge(s_lo[c], used)
                            if c in (2, 3):
                                src, k = self.i["exp_w2"], FT // 2
                                at = (c - 2) * k * P
                            else:
                                src, k = self.i[("exp_w1", "exp_w3")[c % 2]], HK
                                at = (c // 4) * k * P
                            sp.dma_start(w[:, c, :].rearrange("p (k n) -> p k n", k=k),
                                         src[layer, bass.ds(e, 1), at:at + k * P, :].rearrange("a (k p) n -> p (a k) n", p=P)
                                         ).then_inc(s_w[c], 16)

                    if used is None:
                        load()
                        return
                    before = sp.value_load(self.table[0:1, bass.ds(m - 1, 1)], min_val=0, max_val=NE - 1)
                    with sp.If(before < e):
                        load()
                    with sp.If(e < before + 1):
                        for c in chunks:
                            sp.wait_ge(s_lo[c], used)
                            sp.sem_inc(s_w[c], 16)

                def body(j, u, left):
                    b = 2 * j + u
                    if left >= 2:
                        sp.wait_ge(s_tx, 2 * b + 2)
                        rows(b + 2, u)
                        weights(b + 2, (0, 1), b + 2)
                    if left >= 1:
                        weights(b + 1, (2, 3), b + 1)
                    if left >= 2:
                        weights(b + 2, (4, 5), b + 2)

                rows(0, 0)
                weights(0, (0, 1), None)
                rows(1, 1)
                weights(0, (4, 5), None)
                weights(1, (0, 1), 1)
                weights(0, (2, 3), None)
                weights(1, (4, 5), 1)
                over_blocks(sp, body)

            @block.tensor
            def _(pe):
                def three(out, ah, al, bh, bl, first, last):
                    pe.matmul(out, ah, bh, start=first, stop=False)
                    pe.matmul(out, ah, bl, start=False, stop=False)
                    return pe.matmul(out, al, bh, start=False, stop=last)

                def x_part(b, u, c):
                    pe.wait_ge(s_xl, 2 * b + 1 + c // 4)
                    pe.wait_ge(s_lo[c], b + 1)
                    at_slot = slot(c, 1 - u)
                    for k in range(HK):
                        at, to = (c // 4 * HK + k) * P, k * FF
                        ins = three(ph[u][c % 2][:], xh[:, u, at:at + P], xl[:, u, at:at + P], wh[:, at_slot, to:to + FF],
                                    wl[:, at_slot, to:to + FF], first=(c < 2 and k == 0), last=(c >= 4 and k == HK - 1))
                    ins.then_inc(s_c[c], 1)

                def y_part(b, u, c):
                    pe.wait_ge(s_lo[c], b + 1)
                    at_slot = slot(c, u)
                    for q in range(FT // 2):
                        at = ((c - 2) * (FT // 2) + q) * P
                        for half in range(2):
                            to = q * D + half * 512
                            ins = three(py[half][:], gh[:, at:at + P], gl[:, at:at + P], wh[:, at_slot, to:to + 512],
                                        wl[:, at_slot, to:to + 512], first=(at == 0), last=(at == (FT - 1) * P))
                    ins.then_inc(s_c[c], 1)

                def transpose_x(m, u, j, half):
                    if half == 0:
                        pe.wait_ge(s_x[u], 16 * j + 16)
                    if half or not isinstance(m, int) or m:
                        pe.wait_ge(s_xl, 2 * m + half)
                    for k in range(HK):
                        at = (half * HK + k) * P
                        ins = pe.transpose(px[:, k * P:(k + 1) * P], xr[:, u, at:at + P], self.c("ident"))
                    ins.then_inc(s_tx, 1)

                def body(j, u, left):
                    b = 2 * j + u
                    if left >= 1:
                        x_part(b + 1, 1 - u, 0)
                    pe.wait_ge(s_g, b + 1)
                    for k in range(FT):
                        ins = pe.transpose(pg[:, k * P:(k + 1) * P], g[:, k * P:(k + 1) * P], self.c("ident"))
                    ins.then_inc(s_gt, 1)
                    if left >= 1:
                        x_part(b + 1, 1 - u, 1)
                    if left >= 2:
                        transpose_x(b + 2, u, j + 1, 0)
                    pe.wait_ge(s_gl, b + 1)
                    y_part(b, u, 2)
                    y_part(b, u, 3)
                    if left >= 2:
                        transpose_x(b + 2, u, j + 1, 1)
                    if left >= 1:
                        x_part(b + 1, 1 - u, 4)
                        x_part(b + 1, 1 - u, 5)

                transpose_x(0, 0, 0, 0)
                transpose_x(0, 0, 0, 1)
                x_part(0, 0, 0)
                x_part(0, 0, 1)
                transpose_x(1, 1, 0, 0)
                x_part(0, 0, 4)
                transpose_x(1, 1, 0, 1)
                x_part(0, 0, 5)
                last = over_blocks(pe, body)
                pe.wait_ge(s_st, last * 32 + 32 + 16)

            def split_hi(eng, c, cycle, parity):
                free = cycle + 2 if c >= 4 else cycle + 1 if c >= 2 else cycle
                if not isinstance(free, int) or free > 0:
                    eng.wait_ge(s_c[(c - RING) % NC], free)
                eng.wait_ge(s_w[c], 16 * block_of(c, cycle) + 16)
                dst, src = wh[:, slot(c, parity), :], w[:, c, :]
                ins = eng.activation(dst, src, ACT.Copy) if c != 5 else eng.tensor_copy(dst, src)
                ins.then_inc(s_hi[c], 1)

            def split_lo(eng, c, cycle, parity):
                eng.wait_ge(s_hi[c], block_of(c, cycle) + 1)
                at = slot(c, parity)
                eng.tensor_tensor(wl[:, at, :], w[:, c, :], wh[:, at, :].bitcast(F32), ALU.subtract).then_inc(s_lo[c], 1)

            @block.gpsimd
            def _(pool):
                def body(j, u, left):
                    split_lo(pool, 3, 2 * j + u, u)

                over_blocks(pool, body)

            @block.scalar
            def _(act):
                def x_hi(m, u, half):
                    act.wait_ge(s_tx, 2 * m + half + 1)
                    act.activation(xh[:, u, half * 512:half * 512 + 512], px[:], ACT.Copy).then_inc(s_xh, 1)

                def silu(m, u):
                    act.wait_ge(s_c[4], m + 1)
                    if not isinstance(m, int):
                        act.wait_ge(s_g, m)
                    act.activation(sg[:], ph[u][0][:], ACT.Silu).then_inc(s_sg, 1)

                def body(j, u, left):
                    b = 2 * j + u
                    act.wait_ge(s_gt, b + 1)
                    act.activation(gh[:], pg[:], ACT.Copy).then_inc(s_gh, 1)
                    split_hi(act, 3, b, u)
                    if left >= 1:
                        split_hi(act, 4, b, u)
                    if left >= 2:
                        x_hi(b + 2, u, 0)
                        split_hi(act, 0, b + 1, 1 - u)
                        x_hi(b + 2, u, 1)
                        split_hi(act, 1, b + 1, 1 - u)
                    act.wait_ge(s_c[3], b + 1)
                    act.wait_ge(s_st, 16 * b + 16)
                    for half in range(2):
                        ins = act.activation(yr[:, half * 512:(half + 1) * 512], py[half][:], ACT.Copy)
                    ins.then_inc(s_ye, 1)
                    act.wait_ge(s_ye, b + 1)
                    act.dma_start(self.ys[bass.ds(b * P, P), :], yr[:]).then_inc(s_st, 16)
                    if left >= 1:
                        silu(b + 1, 1 - u)
                        split_hi(act, 2, b + 1, 1 - u)

                act.sem_inc(s_st, 16)
                x_hi(0, 0, 0)
                x_hi(0, 0, 1)
                split_hi(act, 0, -1, 1)
                split_hi(act, 1, -1, 1)
                x_hi(1, 1, 0)
                split_hi(act, 4, -1, 1)
                x_hi(1, 1, 1)
                split_hi(act, 0, 0, 0)
                split_hi(act, 1, 0, 0)
                silu(0, 0)
                split_hi(act, 2, 0, 0)
                over_blocks(act, body)

            @block.vector
            def _(dve):
                def x_lo(m, u, half):
                    cols = slice(half * 512, half * 512 + 512)
                    dve.wait_ge(s_xh, 2 * m + half + 1)
                    dve.tensor_tensor(xl[:, u, cols], px[:], xh[:, u, cols].bitcast(F32), ALU.subtract).then_inc(s_xl, 1)

                def body(j, u, left):
                    b = 2 * j + u
                    dve.wait_ge(s_sg, b + 1)
                    dve.wait_ge(s_c[5], b + 1)
                    dve.tensor_tensor(g[:], sg[:], ph[u][1][:], ALU.mult).then_inc(s_g, 1)
                    split_lo(dve, 2, b, u)
                    dve.wait_ge(s_gh, b + 1)
                    dve.tensor_tensor(gl[:], pg[:], gh[:].bitcast(F32), ALU.subtract).then_inc(s_gl, 1)
                    if left >= 1:
                        split_lo(dve, 4, b, u)
                    if left >= 2:
                        x_lo(b + 2, u, 0)
                    if left >= 1:
                        split_hi(dve, 5, b, u)
                        split_lo(dve, 5, b, u)
                    if left >= 2:
                        split_lo(dve, 0, b + 1, 1 - u)
                        x_lo(b + 2, u, 1)
                        split_lo(dve, 1, b + 1, 1 - u)

                x_lo(0, 0, 0)
                x_lo(0, 0, 1)
                split_lo(dve, 0, -1, 1)
                split_lo(dve, 1, -1, 1)
                x_lo(1, 1, 0)
                split_lo(dve, 4, -1, 1)
                x_lo(1, 1, 1)
                split_hi(dve, 5, -1, 1)
                split_lo(dve, 5, -1, 1)
                split_lo(dve, 0, 0, 0)
                split_lo(dve, 1, 0, 0)
                over_blocks(dve, body)

    def combine(self, layer, nt):
        nc = self.nc
        NB = 3
        with ExitStack() as ctx:
            ya = self.sb(ctx, "y_a", [P, NB, D])
            yb = self.sb(ctx, "y_b", [P, NB, D])
            pt = [self.ps(ctx, f"pt{i}", [P, 2 * 512]) for i in range(2)]
            s_ya, s_yb = ([self.sem(ctx, f"c_{n}{i}") for i in range(NB)] for n in ("ya", "yb"))
            s_wa, s_wb, s_t, s_x = (self.sem(ctx, "c_" + n) for n in ("wa", "wb", "t", "xx"))
            block = ctx.enter_context(nc.Block())

            @block.gpsimd
            def _(pool):
                for t in range(nt):
                    if t >= NB:
                        pool.wait_ge(s_t, t - NB + 1)
                    for c, (y, sem) in enumerate(((ya, s_ya), (yb, s_yb))):
                        pool.indirect_dma_start(y[:, t % NB, :], None, self.ys,
                                                bass.IndirectOffsetOnAxis(self.slot[:, c, t:t + 1], 0)).then_inc(sem[t % NB], 16)

            @block.scalar
            def _(act):
                for t in range(nt):
                    act.wait_ge(s_ya[t % NB], 16 * (t // NB + 1))
                    act.activation(ya[:, t % NB, :], ya[:, t % NB, :], ACT.Copy, scale=self.wgt[:, 0, t:t + 1]).then_inc(s_wa, 1)

            @block.vector
            def _(dve):
                for t in range(nt + 1):
                    if t < nt:
                        dve.wait_ge(s_wa, t + 1)
                        dve.wait_ge(s_yb[t % NB], 16 * (t // NB + 1))
                        dve.scalar_tensor_tensor(yb[:, t % NB, :], yb[:, t % NB, :], self.wgt[:, 1, t:t + 1], ya[:, t % NB, :],
                                                 ALU.mult, ALU.add).then_inc(s_wb, 1)
                    if t:
                        dve.wait_ge(s_t, t)
                        at = (t - 1) * P
                        for k in range(KT):
                            ins = dve.scalar_tensor_tensor(self.xT[:, k, at:at + P], pt[(t - 1) % 2][:, k * P:(k + 1) * P],
                                                           self.mods[:, layer, 5, k, int(t > LT):int(t > LT) + 1],
                                                           self.xT[:, k, at:at + P], ALU.mult, ALU.add)
                        ins.then_inc(s_x, 1)

            @block.tensor
            def _(pe):
                for t in range(nt):
                    pe.wait_ge(s_wb, t + 1)
                    if t >= 2:
                        pe.wait_ge(s_x, t - 1)
                    for k in range(KT):
                        ins = pe.transpose(pt[t % 2][:, k * P:(k + 1) * P], yb[:, t % NB, k * P:(k + 1) * P], self.c("ident"))
                    ins.then_inc(s_t, 1)

    def layer_odd(self):
        with ExitStack() as ctx:
            self.Y = self.sb(ctx, "Y", [P, 2 * BR, SEQ])
            self.odd_mixer()
            self.merge(1, LT)

    def odd_mixer(self):
        nc = self.nc
        WC = 3 * P
        GAP = LRU_ROW - 3 - CTX
        L = LRU_ROW - 3
        PAD = 8
        unit = [(i, kind, c) for i in range(BR) for kind in ("ux", "ug", "up") for c in range(3 if kind == "ux" else 2)]
        with ExitStack() as ctx:
            hT = self.sb(ctx, "hT", [P, KT, TOK])
            w = self.sb(ctx, "w_cd", [P, 2, KT, WC])
            gw = self.sb(ctx, "gate_w", [P, 2, 2, BR, P])
            pw = self.sb(ctx, "pool_weights", [P, BR, P])
            up = self.sb(ctx, "u_pad", [P, LRU_ROW])
            xl = self.sb(ctx, "x_conv", [P, L])
            lanes = [[self.sb(ctx, f"lru{d}{n}", [P, L]) for n in range(3)] for d in range(2)]
            sqr = self.sb(ctx, "a_squared", [P, L])
            pp = [self.sb(ctx, f"pool{n}", [P, PAD + SEQ + PAD]) for n in range(2)]
            z = [self.ps(ctx, f"z{i}", [P, 512]) for i in range(2)]
            pa, pxg = self.ps(ctx, "pa", [P, 3 * 512]), self.ps(ctx, "pxg", [P, 3 * 512])
            nrm = self.norm_open(ctx, "n1", NT)
            s_w = [self.sem(ctx, f"o_w{i}") for i in range(2)]
            (s_gw, s_pw, s_zero, s_z, s_ux, s_ug, s_up, s_cv, s_pg, s_r, s_a, s_q, s_sq, s_b, s_h, s_gu, s_y, s_pl, s_pd,
             s_pm, s_pe, s_ch) = (
                self.sem(ctx, "o_" + n) for n in ("gw", "pw", "zero", "z", "ux", "ug", "up", "cv", "pg", "r", "a", "q", "sqr",
                                                  "b", "h", "gu", "y", "pl", "pd", "pm", "pe", "ch"))
            block = ctx.enter_context(nc.Block())
            W = self.i["w_in_cd"][0].rearrange("(k p) n -> p k n", p=P)
            both = ((0, 0, SEQ), (SEQ, GAP, CTX))

            def wait_z_read(eng, n):
                i, kind, c = unit[n]
                if kind == "ux":
                    eng.wait_ge(s_ux, 3 * i + c + 1)
                else:
                    eng.wait_ge({"ug": s_ug, "up": s_up}[kind], 2 * i + c + 1)

            @block.sync
            def _(sp):
                sp.wait_ge(s_zero, 1)
                for d in range(2):
                    for gate, name in enumerate(("lru_wa", "lru_wx")):
                        for par in range(2):
                            sp.dma_start(gw[par * HD:(par + 1) * HD, d, gate, :, par * HD:(par + 1) * HD],
                                         self.i[name][0, d, par::2, :, :].rearrange("i h j -> h i j")).then_inc(s_gw, 16)
                sp.dma_start(pw[:], self.i["pool_w"][0].rearrange("g i j -> i g j")).then_inc(s_pw, 16)
                for i in range(BR):
                    if i >= 2:
                        sp.wait_ge(s_z, 7 * (i - 1))
                    for g, base in enumerate((0, SC_W, 2 * SC_W)):
                        sp.dma_start(w[:, i % 2, :, g * P:(g + 1) * P], W[:, :, base + i * P:base + (i + 1) * P]
                                     ).then_inc(s_w[i % 2], 16)

            @block.tensor
            def _(pe):
                self.norm_pe(pe, nrm, hT, z[0], pa)

                def gates(i, d):
                    k = 2 * i + d
                    pe.wait_ge(s_cv, i + 1)
                    if k:
                        pe.wait_ge(s_r, 2 * k)
                    for gate, ps in enumerate((pa, pxg)):
                        for at, size in CHUNKS:
                            to = at if at < SEQ else GAP
                            ins = pe.matmul(ps[:, at:at + size], gw[:, d, gate, i, :], xl[:, to:to + size],
                                            start=True, stop=True)
                    ins.then_inc(s_pg, 1)

                def pool_product(i, c, n):
                    pe.wait_ge(s_pd, i + 1)
                    wait_z_read(pe, n)
                    pe.matmul(z[n % 2][:], pw[:, i, :], pp[0][:, PAD + c * 512:PAD + (c + 1) * 512],
                              start=True, stop=True).then_inc(s_pm, 1)

                pe.wait_ge(s_gw, 16 * 8)
                pe.wait_ge(s_pw, 16)
                for n, (i, kind, c) in enumerate(unit):
                    if kind == "ux" and c == 0:
                        pe.wait_ge(s_w[i % 2], 48 * (i // 2 + 1))
                    if n >= 2:
                        wait_z_read(pe, n - 2)
                    if kind == "ug" and i:
                        pe.wait_ge(s_pe, 2 * i)
                    at, size = CHUNKS[c]
                    to = ("ux", "ug", "up").index(kind) * P
                    for k in range(KT):
                        if n == 0:
                            pe.wait_ge(nrm["h"], k + 1)
                        ins = pe.matmul(z[n % 2][:, 0:size], w[:, i % 2, k, to:to + P], hT[:, k, at:at + size],
                                        start=(k == 0), stop=(k == KT - 1))
                    ins.then_inc(s_z, 1)
                    if kind == "ug" and c == 1:
                        gates(i, 0)
                    if kind == "up" and c == 1:
                        gates(i, 1)
                    if kind == "ux" and c in (1, 2) and i:
                        pool_product(i - 1, c - 1, n)
                pool_product(BR - 1, 0, len(unit) - 2)
                pool_product(BR - 1, 1, len(unit) - 1)

            @block.scalar
            def _(act):
                self.norm_act(act, nrm, hT, 1, 0)

                def pool_out(i, c, n):
                    act.wait_ge(s_pm, 2 * i + c + 1)
                    act.activation(self.Y[:, i, c * 512:(c + 1) * 512], z[n % 2][:], ACT.Copy,
                                   scale=self.param("pool_scale", i)).then_inc(s_pe, 1)

                def gate_out(i, d):
                    k = 2 * i + d
                    R, G, S = lanes[d]
                    act.wait_ge(s_pg, k + 1)
                    if i:
                        act.wait_ge(s_y, i)
                    for gate, (dst, ps, name) in enumerate(((R, pa, "lru_ba"), (G, pxg, "lru_bx"))):
                        for at, to, size in both:
                            ins = act.activation(dst[:, to:to + size], ps[:, at:at + size], ACT.Sigmoid,
                                                 bias=self.param(name, d * BR + i))
                        ins.then_inc(s_r, 1)
                    act.wait_ge(s_r, 2 * k + 2)
                    for at, to, size in both:
                        ins = act.activation(S[:, to:to + size], R[:, to:to + size], ACT.Tanh,
                                             scale=self.decay[:, 1, d * BR + i:d * BR + i + 1])
                    ins.then_inc(s_ch, 1)
                    act.wait_ge(s_ch, k + 1)
                    for at, to, size in both:
                        ins = act.activation(R[:, to:to + size], R[:, to:to + size], ACT.Exp,
                                             scale=self.decay[:, 0, d * BR + i:d * BR + i + 1])
                    ins.then_inc(s_a, 1)

                def root(i, d):
                    k = 2 * i + d
                    S = lanes[d][2]
                    act.wait_ge(s_q, k + 1)
                    for at, to, size in both:
                        ins = act.activation(S[:, to:to + size], S[:, to:to + size], ACT.Sqrt)
                    ins.then_inc(s_sq, 1)

                for n, (i, kind, c) in enumerate(unit):
                    act.wait_ge(s_z, n + 1)
                    at, size = CHUNKS[c]
                    if kind == "ux":
                        if c == 0:
                            act.wait_ge(s_zero, 2)
                            if i:
                                act.wait_ge(s_cv, i)
                        to = 2 + at if at < SEQ else 2 + GAP
                        act.activation(up[:, to:to + size], z[n % 2][:, 0:size], ACT.Copy).then_inc(s_ux, 1)
                        if c and i:
                            pool_out(i - 1, c - 1, n)
                    elif kind == "ug":
                        act.activation(self.Y[:, BR + i, at:at + size], z[n % 2][:], ACT.Gelu_apprx_tanh).then_inc(s_ug, 1)
                        if c == 1:
                            gate_out(i, 0)
                    else:
                        if c == 0 and i:
                            act.wait_ge(s_pm, 2 * i)
                        act.activation(pp[0][:, PAD + at:PAD + at + size], z[n % 2][:], ACT.Copy).then_inc(s_up, 1)
                        if c == 1:
                            root(i, 0)
                            gate_out(i, 1)
                            root(i, 1)
                for c in range(2):
                    pool_out(BR - 1, c, len(unit) - 2 + c)

            @block.vector
            def _(dve):
                dve.memset(gw[:], 0.0).then_inc(s_zero, 1)
                for buf in (up, *pp, *(b for lane in lanes for b in lane)):
                    ins = dve.memset(buf[:], 0.0)
                ins.then_inc(s_zero, 1)
                dve.wait_ge(s_zero, 2)
                self.norm_dve(dve, nrm, hT, z[0], pa)
                link = Chain(dve, s_h)
                for i in range(BR):
                    dve.wait_ge(s_ux, 3 * i + 3)
                    if i:
                        dve.wait_ge(s_pg, 2 * i)
                        dve.wait_ge(s_gu, 2 * i)
                    link.step(dve.tensor_scalar(xl[:], up[:, 0:L], self.param("lru_conv_w", i), self.param("lru_conv_b", i),
                                                ALU.mult, ALU.add))
                    for k in (1, 2, 3):
                        ins = dve.scalar_tensor_tensor(xl[:], up[:, k:k + L], self.param("lru_conv_w", k * BR + i), xl[:],
                                                       ALU.mult, ALU.add)
                        link.step(ins)
                    dve.engine_nop().then_inc(s_cv, 1)
                    for d in range(2):
                        k = 2 * i + d
                        R, G, S = lanes[d]
                        dve.wait_ge(s_a, k + 1)
                        link.step(dve.tensor_tensor(sqr[:], R[:], R[:], ALU.mult))
                        dve.scalar_tensor_tensor(S[:], sqr[:], 1.0, S[:], ALU.add, ALU.mult).then_inc(s_q, 1)
                        dve.wait_ge(s_q, k + 1)
                        dve.wait_ge(s_gu, k + 1)
                        dve.wait_ge(s_sq, k + 1)
                        link.step(dve.tensor_tensor(S[:], S[:], G[:], ALU.mult))
                        lat, ctxs = slice(0, SEQ), slice(GAP, GAP + CTX)
                        flip = (lambda ap: ap[:, ::-1]) if d else (lambda ap: ap)
                        link.step(dve.tensor_tensor_scan(flip(G[:, ctxs]), flip(R[:, ctxs]), flip(S[:, ctxs]), 0.0,
                                                         ALU.mult, ALU.add))
                        first = G[:, GAP:GAP + 1] if d else G[:, GAP + CTX - 1:GAP + CTX]
                        link.step(dve.tensor_tensor_scan(flip(G[:, lat]), flip(R[:, lat]), flip(S[:, lat]), first,
                                                         ALU.mult, ALU.add))
                    link.step(dve.tensor_tensor(lanes[0][1][:, 0:SEQ], lanes[0][1][:, 0:SEQ], lanes[1][1][:, 0:SEQ], ALU.add))
                    dve.wait_ge(s_ug, 2 * i + 2)
                    dve.tensor_tensor(self.Y[:, BR + i, :], self.Y[:, BR + i, :], lanes[0][1][:, 0:SEQ], ALU.mult
                                      ).then_inc(s_y, 1)
                    dve.wait_ge(s_y, i + 1)

            @block.gpsimd
            def _(pool):
                n_pl = [0]

                def step(ins):
                    n_pl[0] += 1
                    ins.then_inc(s_pl, 1)
                    pool.wait_ge(s_pl, n_pl[0])

                pool.wait_ge(s_zero, 2)
                for i in range(BR):
                    for d in range(2):
                        k = 2 * i + d
                        pool.wait_ge(s_r, 2 * k + 2)
                        G = lanes[d][1]
                        pool.tensor_tensor(G[:], G[:], xl[:], ALU.mult).then_inc(s_gu, 1)
                        if d == 0:
                            pool.wait_ge(s_up, 2 * i + 2)
                            win = POOL_WINDOWS[i]
                            src, sums, size, width = pp[0], pp[1], PAD + SEQ + PAD, 1
                            while width < win:
                                size -= width
                                step(pool.tensor_tensor(sums[:, 0:size], src[:, 0:size], src[:, width:width + size], ALU.add))
                                src, width = sums, 2 * width
                            at = PAD - win // 2
                            step(pool.tensor_scalar(sums[:, 0:SEQ], sums[:, at:at + SEQ], 1.0 / win, None, ALU.mult))
                            for e, to in enumerate((0, SEQ - 8)):
                                edge = self.const[:, COL["edges"] + 16 * i + 8 * e:COL["edges"] + 16 * i + 8 * e + 8]
                                step(pool.tensor_tensor(sums[:, to:to + 8], sums[:, to:to + 8], edge, ALU.mult))
                            pool.tensor_tensor(pp[0][:, PAD:PAD + SEQ], sums[:, 0:SEQ], pp[0][:, PAD:PAD + SEQ],
                                               ALU.subtract).then_inc(s_pd, 1)

    def epilogue(self):
        nc = self.nc
        with ExitStack() as ctx:
            rows = self.sb(ctx, "out_rows", [P, 2, D])
            pt = [self.ps(ctx, f"pt{i}", [P, 2 * 512]) for i in range(2)]
            s_t, s_e = self.sem(ctx, "f_t"), self.sem(ctx, "f_e")
            s_o = [self.sem(ctx, f"f_o{i}") for i in range(2)]
            block = ctx.enter_context(nc.Block())

            @block.tensor
            def _(pe):
                for t in range(LT):
                    if t >= 2:
                        pe.wait_ge(s_e, t - 1)
                    for k in range(KT):
                        ins = pe.transpose(pt[t % 2][:, k * P:(k + 1) * P], self.xT[:, k, t * P:(t + 1) * P], self.c("ident"))
                    ins.then_inc(s_t, 1)

            @block.scalar
            def _(act):
                for t in range(LT):
                    act.wait_ge(s_t, t + 1)
                    if t >= 2:
                        act.wait_ge(s_o[t % 2], 16 * (t // 2))
                    act.activation(rows[:, t % 2, :], pt[t % 2][:, :], ACT.Copy).then_inc(s_e, 1)

            @block.sync
            def _(sp):
                for t in range(LT):
                    sp.wait_ge(s_e, t + 1)
                    sp.dma_start(self.out[0, t * P:(t + 1) * P, :], rows[:, t % 2, :]).then_inc(s_o[t % 2], 16)
                for i in range(2):
                    sp.wait_ge(s_o[i], 16 * LT // 2)


_INS = ["x", "c", "ctx", "c_ctx", "ada_w", "ada_b", "norm_mix", "norm_ffn", "out_norm", "w_out", "w_in_ab", "q_norm",
        "k_norm", "attn_sink", "sconv_w", "sconv_b", "w_in_cd", "pool_w", "pool_scale", "lru_conv_w", "lru_conv_b",
        "lru_wa", "lru_ba", "lru_wx", "lru_bx", "lru_lambda", "router_gw", "router_gb", "router_ew", "router_eb",
        "exp_w1", "exp_w3", "exp_w2"]


def build(nc, ins, out):
    Program(nc, ins, out).build()


def kernel(**inputs):
    import numpy as _np
    import concourse.bacc as _bacc
    from concourse import mybir as _mybir
    from concourse.bass_utils import run_bass_kernel_spmd as _run

    nc = _bacc.Bacc("TRN2", target_bir_lowering=False, num_devices=1)
    arrays = {f"in_{name}": _np.ascontiguousarray(inputs[name]) for name in _INS}
    arrays.update((f"in_{name}", a) for name, a in shape_constants().items())
    ins = {name[3:]: nc.dram_tensor(name, a.shape, _mybir.dt.from_np(a.dtype), kind="ExternalInput").ap()
           for name, a in arrays.items()}
    out = nc.dram_tensor("out", (1, SEQ, D), _mybir.dt.float32, kind="ExternalOutput").ap()
    build(nc, ins, out)
    return _run(nc, [arrays], core_ids=[0]).results[0]["out"]
```
